# Optimizing a Trainium2 kernel written in Bass

```python
import math
import jax, jax.numpy as jnp
from jax import lax
import numpy as np

D_MODEL = 2048
BATCH = 1
SEQ = 512
DEPTH = 1
DEC_BATCH = 8
DEC_SEQ = 8
PAST_LEN = 4096
PAGE_SIZE = 128

H_RET = 4
DK_RET = 128
DV_RET = 256
H_GLA = 4
DK_GLA = 128
DV_GLA = 256
GLA_RANK = 16
GLA_TEMP = 16.0
D_MIX = H_RET * DV_RET + H_GLA * DV_GLA
CHUNK = 64
ROPE_BASE = 10000.0
PEER_HEADS = 8
PEER_NKEYS = 128
PEER_DQ = 256
PEER_TOPK = 16
PEER_BLOCK = 128
N_EXPERTS = PEER_NKEYS * PEER_NKEYS
EPS = 1e-6

IN_SPLITS = (H_RET * DK_RET, H_RET * DK_RET, H_RET * DV_RET, H_RET * DV_RET,
             H_GLA * DK_GLA, H_GLA * DK_GLA, H_GLA * DV_GLA, H_GLA * DV_GLA, GLA_RANK)
D_IN = sum(IN_SPLITS)
IN_CUTS = tuple(int(c) for c in np.cumsum(IN_SPLITS)[:-1])

kernel_name = "hymba_retnet_gla_peer_step"

def rmsnorm(x, w):
    xf = x.astype(jnp.float32)
    y = xf * lax.rsqrt(jnp.mean(xf * xf, axis=-1, keepdims=True) + EPS)
    return (y * w.astype(jnp.float32)).astype(x.dtype)

def group_norm_heads(o, w, b):
    mu = jnp.mean(o, axis=-1, keepdims=True)
    var = jnp.mean(jnp.square(o - mu), axis=-1, keepdims=True)
    return (o - mu) * lax.rsqrt(var + EPS) * w.astype(jnp.float32) + b.astype(jnp.float32)

def rms_norm_heads(o, w):
    return o * lax.rsqrt(jnp.mean(o * o, axis=-1, keepdims=True) + EPS) * w.astype(jnp.float32)

def rotary(x, pos):
    d = x.shape[-1]
    freqs = ROPE_BASE ** (-jnp.arange(0, d, 2, dtype=jnp.float32) / d)
    ang = pos[:, None] * freqs[None, :]
    cos = jnp.cos(ang)[None, :, None, :]
    sin = jnp.sin(ang)[None, :, None, :]
    x1, x2 = x[..., : d // 2], x[..., d // 2:]
    return jnp.concatenate([x1 * cos - x2 * sin, x1 * sin + x2 * cos], axis=-1)

def to_chunks(t, c):
    b, l, h, d = t.shape
    return t.reshape(b, l // c, c, h, d).transpose(1, 0, 3, 2, 4)

def from_chunks(t):
    n, b, h, c, d = t.shape
    return t.transpose(1, 0, 3, 2, 4).reshape(b, n * c, h, d)

def retention_chunkwise(q, k, v, s0):
    L = q.shape[1]
    c = math.gcd(L, CHUNK)
    log_g = jnp.log1p(-jnp.exp2(-5.0 - jnp.arange(H_RET, dtype=jnp.float32)))
    idx = jnp.arange(c, dtype=jnp.float32)
    dist = idx[:, None] - idx[None, :]
    causal = dist >= 0
    decay_mask = jnp.where(causal[None], jnp.exp(jnp.maximum(dist, 0.0)[None] * log_g[:, None, None]), 0.0)
    q_decay = jnp.exp((idx + 1.0)[None, :] * log_g[:, None])
    k_decay = jnp.exp((c - 1.0 - idx)[None, :] * log_g[:, None])
    chunk_decay = jnp.exp(c * log_g)

    def step(S, inp):
        qc, kc, vc = inp
        scores = jnp.einsum('bhid,bhjd->bhij', qc, kc) * decay_mask[None]
        inner = jnp.einsum('bhij,bhjv->bhiv', scores, vc)
        cross = jnp.einsum('bhid,bhdv->bhiv', qc, S) * q_decay[None, :, :, None]
        S_new = S * chunk_decay[None, :, None, None] + jnp.einsum(
            'bhjd,bhjv->bhdv', kc * k_decay[None, :, :, None], vc)
        return S_new, inner + cross

    S_fin, o = lax.scan(step, s0, (to_chunks(q, c), to_chunks(k, c), to_chunks(v, c)))
    return from_chunks(o), S_fin

def gla_chunked(q, k, v, log_a, s0):
    L = q.shape[1]
    c = math.gcd(L, CHUNK)
    causal = jnp.tril(jnp.ones((c, c), dtype=bool))

    def step(S, inp):
        qc, kc, vc, lac = inp
        bcum = jnp.cumsum(lac, axis=2)
        diff = bcum[:, :, :, None, :] - bcum[:, :, None, :, :]
        m = causal[None, None, :, :, None]
        decay = jnp.where(m, jnp.exp(jnp.where(m, diff, 0.0)), 0.0)
        A = jnp.sum(qc[:, :, :, None, :] * kc[:, :, None, :, :] * decay, axis=-1)
        inner = jnp.einsum('bhij,bhjv->bhiv', A, vc)
        cross = jnp.einsum('bhid,bhdv->bhiv', qc * jnp.exp(bcum), S)
        b_last = bcum[:, :, -1:, :]
        S_new = S * jnp.exp(b_last[:, :, 0, :])[..., None] + jnp.einsum(
            'bhjd,bhjv->bhdv', kc * jnp.exp(b_last - bcum), vc)
        return S_new, inner + cross

    S_fin, o = lax.scan(step, s0, (to_chunks(q, c), to_chunks(k, c), to_chunks(v, c), to_chunks(log_a, c)))
    return from_chunks(o), S_fin

def mixer_block(x, pos, s_ret0, s_gla0, w_norm_mix, w_in, w_gla_a2, b_gla_a,
                gn_ret_w, gn_ret_b, gn_gla_w, w_out):
    B, L, _ = x.shape
    h = rmsnorm(x, w_norm_mix)
    proj = jnp.einsum('bld,de->ble', h, w_in).astype(jnp.float32)
    q_r, k_r, v_r, g_r, q_g, k_g, v_g, g_g, a_lr = jnp.split(proj, IN_CUTS, axis=-1)
    q_r = rotary(q_r.reshape(B, L, H_RET, DK_RET), pos)
    k_r = rotary(k_r.reshape(B, L, H_RET, DK_RET), pos) * (DK_RET ** -0.5)
    o_r, s_ret = retention_chunkwise(q_r, k_r, v_r.reshape(B, L, H_RET, DV_RET), s_ret0.astype(jnp.float32))
    o_r = group_norm_heads(o_r, gn_ret_w, gn_ret_b).reshape(B, L, H_RET * DV_RET) * jax.nn.silu(g_r)
    log_a = jax.nn.log_sigmoid(jnp.einsum('blr,re->ble', a_lr, w_gla_a2.astype(jnp.float32))
                               + b_gla_a.astype(jnp.float32)) / GLA_TEMP
    q_g = q_g.reshape(B, L, H_GLA, DK_GLA) * (DK_GLA ** -0.5)
    o_g, s_gla = gla_chunked(q_g, k_g.reshape(B, L, H_GLA, DK_GLA), v_g.reshape(B, L, H_GLA, DV_GLA),
                             log_a.reshape(B, L, H_GLA, DK_GLA), s_gla0.astype(jnp.float32))
    o_g = rms_norm_heads(o_g, gn_gla_w).reshape(B, L, H_GLA * DV_GLA) * jax.nn.silu(g_g)
    mix = jnp.concatenate([o_r, o_g], axis=-1).astype(x.dtype)
    return x + jnp.einsum('ble,ed->bld', mix, w_out), s_ret, s_gla

def peer_block(x, w_norm_ffn, w_pq, sub_keys1, sub_keys2, u_tab, v_tab):
    B, L, D = x.shape
    h = rmsnorm(x, w_norm_ffn).reshape(B * L, D)
    T = B * L
    Tp = -(-T // PEER_BLOCK) * PEER_BLOCK
    hb = jnp.pad(h, ((0, Tp - T), (0, 0))).reshape(Tp // PEER_BLOCK, PEER_BLOCK, D)

    def one_block(xb):
        q = jnp.einsum('td,de->te', xb, w_pq).astype(jnp.float32).reshape(
            PEER_BLOCK, PEER_HEADS, 2, PEER_DQ // 2)
        s1 = jnp.einsum('thd,hnd->thn', q[:, :, 0], sub_keys1.astype(jnp.float32))
        s2 = jnp.einsum('thd,hnd->thn', q[:, :, 1], sub_keys2.astype(jnp.float32))
        v1, i1 = lax.top_k(s1, PEER_TOPK)
        v2, i2 = lax.top_k(s2, PEER_TOPK)
        cand_s = (v1[..., :, None] + v2[..., None, :]).reshape(PEER_BLOCK, PEER_HEADS, PEER_TOPK * PEER_TOPK)
        cand_i = (i1[..., :, None] * PEER_NKEYS + i2[..., None, :]).reshape(PEER_BLOCK, PEER_HEADS, PEER_TOPK * PEER_TOPK)
        top_s, sel = lax.top_k(cand_s, PEER_TOPK)
        eidx = jnp.take_along_axis(cand_i, sel, axis=-1)
        gate = jax.nn.softmax(top_s, axis=-1)
        u = u_tab[eidx]
        act = jax.nn.gelu(jnp.einsum('thkd,td->thk', u, xb).astype(jnp.float32), approximate=False)
        return jnp.einsum('thk,thkd->td', (gate * act).astype(xb.dtype), v_tab[eidx])

    out = lax.map(one_block, hb).reshape(Tp, D)[:T].reshape(B, L, D)
    return x + out.astype(x.dtype)

def setup_inputs(seed: int = 0) -> dict:
    key = jax.random.key(seed)
    ks = jax.random.split(key, 20)
    n = jax.random.normal
    f32 = jnp.float32
    return {
        "x_prompt": n(ks[0], (BATCH, SEQ, D_MODEL), f32),
        "x_sample": n(ks[1], (DEC_BATCH, DEC_SEQ, D_MODEL), f32),
        "state_ret": 0.5 * n(ks[2], (DEPTH, DEC_BATCH, H_RET, DK_RET, DV_RET), f32),
        "state_gla": 0.5 * n(ks[3], (DEPTH, DEC_BATCH, H_GLA, DK_GLA, DV_GLA), f32),
        "w_norm_mix": 1.0 + 0.01 * n(ks[4], (DEPTH, D_MODEL), f32),
        "w_in": n(ks[5], (DEPTH, D_MODEL, D_IN), f32) * D_MODEL ** -0.5,
        "w_gla_a2": n(ks[6], (DEPTH, GLA_RANK, H_GLA * DK_GLA), f32) * GLA_RANK ** -0.5,
        "b_gla_a": 0.1 * n(ks[7], (DEPTH, H_GLA * DK_GLA), f32),
        "gn_ret_w": 1.0 + 0.01 * n(ks[8], (DEPTH, H_RET, DV_RET), f32),
        "gn_ret_b": 0.01 * n(ks[9], (DEPTH, H_RET, DV_RET), f32),
        "gn_gla_w": 1.0 + 0.01 * n(ks[10], (DEPTH, H_GLA, DV_GLA), f32),
        "w_out": n(ks[11], (DEPTH, D_MIX, D_MODEL), f32) * D_MIX ** -0.5,
        "w_norm_ffn": 1.0 + 0.01 * n(ks[12], (DEPTH, D_MODEL), f32),
        "w_pq": n(ks[13], (DEPTH, D_MODEL, PEER_HEADS * PEER_DQ), f32) * D_MODEL ** -0.5,
        "sub_keys1": n(ks[14], (DEPTH, PEER_HEADS, PEER_NKEYS, PEER_DQ // 2), f32) * (PEER_DQ // 2) ** -0.5,
        "sub_keys2": n(ks[15], (DEPTH, PEER_HEADS, PEER_NKEYS, PEER_DQ // 2), f32) * (PEER_DQ // 2) ** -0.5,
        "u_tab": n(ks[16], (DEPTH, N_EXPERTS, D_MODEL), f32) * D_MODEL ** -0.5,
        "v_tab": 0.5 * n(ks[17], (DEPTH, N_EXPERTS, D_MODEL), f32),
        "w_norm_final": 1.0 + 0.01 * n(ks[18], (D_MODEL,), f32),
    }

def reference(x_prompt, x_sample, state_ret, state_gla, w_norm_mix, w_in, w_gla_a2, b_gla_a,
              gn_ret_w, gn_ret_b, gn_gla_w, w_out, w_norm_ffn, w_pq, sub_keys1, sub_keys2,
              u_tab, v_tab, w_norm_final):
    Bp, Lp, _ = x_prompt.shape
    Bs, Ls, _ = x_sample.shape
    pos_p = jnp.arange(Lp, dtype=jnp.float32)
    pos_s = PAST_LEN + jnp.arange(Ls, dtype=jnp.float32)
    hp, hs = x_prompt, x_sample
    rp_list, gp_list, rs_list, gs_list = [], [], [], []
    for l in range(DEPTH):
        mix_w = (w_norm_mix[l], w_in[l], w_gla_a2[l], b_gla_a[l], gn_ret_w[l], gn_ret_b[l], gn_gla_w[l], w_out[l])
        zero_r = jnp.zeros((Bp, H_RET, DK_RET, DV_RET), jnp.float32)
        zero_g = jnp.zeros((Bp, H_GLA, DK_GLA, DV_GLA), jnp.float32)
        hp, rp, gp = mixer_block(hp, pos_p, zero_r, zero_g, *mix_w)
        hs, rs, gs = mixer_block(hs, pos_s, state_ret[l], state_gla[l], *mix_w)
        ffn_w = (w_norm_ffn[l], w_pq[l], sub_keys1[l], sub_keys2[l], u_tab[l], v_tab[l])
        hp = peer_block(hp, *ffn_w)
        hs = peer_block(hs, *ffn_w)
        rp_list.append(rp)
        gp_list.append(gp)
        rs_list.append(rs)
        gs_list.append(gs)
    y_prompt = rmsnorm(hp, w_norm_final)
    y_sample = rmsnorm(hs, w_norm_final)
    return (y_prompt, y_sample, jnp.stack(rp_list), jnp.stack(gp_list), jnp.stack(rs_list), jnp.stack(gs_list))


_drawn_inputs = setup_inputs


def setup_inputs(seed=0):
    import zlib

    import numpy as np

    out = dict(_drawn_inputs(seed))
    spreads = {}
    factors = {'gn_ret_w': 131.441,
     'gn_ret_b': 123.162,
     'gn_gla_w': 130.406,
     'w_norm_final': 182.834,
     'w_norm_ffn': 34.981}
    for name, (base, spread) in spreads.items():
        noise = np.random.default_rng([zlib.crc32(name.encode()), seed]).standard_normal(out[name].shape)
        drawn = base * np.exp(spread * noise) if base else spread * noise
        out[name] = __import__('jax').numpy.asarray(drawn.astype(out[name].dtype))
    for name, factor in factors.items():
        out[name] = (out[name] * factor).astype(out[name].dtype)
    return out
```

```python
from contextlib import ExitStack

import numpy as np

import concourse.bass as bass
from concourse import mybir

F32 = mybir.dt.float32
F32R = mybir.dt.float32r
U32 = mybir.dt.uint32
ALU = mybir.AluOpType
ACT = mybir.ActivationFunctionType
AX = mybir.AxisListType

P = 128
D = 2048
KT = D // P
SEQ, NSEQ, LSEQ = 512, 8, 8
NSMP = NSEQ * LSEQ
TILES = SEQ // P + 1
PTILES = TILES - 1
TP = TILES * P
PAST = 4096
EPS = 1e-6
H, DK, DV = 4, 128, 256
RANK, TEMP = 16, 16.0
PROJ = 2 * (2 * H * DK + 2 * H * DV)
NB = 512
KQ = 4
QR, KR, VR, GR, QG, KG, VG, GG = 0, 512, 1024, 2048, 3072, 3584, 4096, 5120
SUB, BLK = 8, 32
LOG_A_MIN = -20.0
EXP_MAX = 80.0
HEADS, NKEYS, TOPK, DQ = 8, 128, 16, 128
HK = HEADS * TOPK
DENSE0 = P
ND = PTILES * P - P + NSMP
NG = ND // 64
CH = 4
NCH = NKEYS // CH
DS = D // 512


GAMMA = [1.0 - 2.0 ** (-5 - h) for h in range(H)]


def wait(eng, sem, value):
    if not (isinstance(value, int) and value <= 0):
        eng.wait_ge(sem, value)


class Steps:

    def __init__(self, eng, sem):
        self.eng, self.sem, self.base, self.n, self.offset = eng, sem, 0, 0, 0

    def __call__(self, ins):
        self.n += 1
        ins.then_inc(self.sem, 1)

    def wait(self):
        self.eng.wait_ge(self.sem, self.base + self.n)

    def at(self, base):
        self.base, self.n = base + self.offset, 0


def bcast(ap, axis, count):
    shape = list(ap.shape)
    shape.insert(axis, count)
    return ap.unsqueeze(axis).broadcast_to(shape)


class Alloc:

    def __init__(self, nc, ctx, name):
        self.nc, self.ctx, self.name, self.sems = nc, ctx, name, []
        ctx.callback(self.clear)

    def clear(self):
        for sem in self.sems:
            self.nc.gpsimd.sem_clear(sem)
        self.nc.all_engine_barrier()

    def sb(self, name, shape, dt=F32):
        return self.ctx.enter_context(self.nc.sbuf_tensor(f"{self.name}_{name}", shape, dt))

    def ps(self, name, shape):
        return self.ctx.enter_context(self.nc.psum_tensor(f"{self.name}_{name}", shape, F32))

    def sem(self, name):
        self.sems.append(self.ctx.enter_context(self.nc.semaphore(f"{self.name}_{name}")))
        return self.sems[-1]


    def gpsimd_dma_sem(self, name):
        return self.nc.alloc_semaphore(f"{self.name}_{name}")


def newton_rsqrt(nc, dve, out, mean, root, tmp):
    dve(nc.vector.reciprocal(out, root))
    dve.wait()
    dve(nc.vector.tensor_tensor(tmp, out, out, ALU.mult))
    dve.wait()
    dve(nc.vector.tensor_tensor(tmp, tmp, mean, ALU.mult))
    dve.wait()
    dve(nc.vector.tensor_scalar(tmp, tmp, -0.5, 1.5, ALU.mult, ALU.add))
    dve.wait()
    dve(nc.vector.tensor_tensor(out, out, tmp, ALU.mult))
    dve.wait()


def norm_transpose(nc, name, hi, lo, ident_dram, src, norm=None, add=None, sum_dst=None, row=None, spill=None):
    with ExitStack() as ctx:
        a = Alloc(nc, ctx, name)
        X = a.sb("x", [P, TILES, D])
        Y = a.sb("y", [P, TILES, D]) if add is not None else None
        junk = a.sb("junk", [P, D]) if norm is not None else None
        xn = a.sb("xn", [P, D])
        ident = a.sb("ident", [P, P])
        wcol = a.sb("wcol", [P, KT])
        mean = a.sb("mean", [P, TILES])
        root = a.sb("root", [P, TILES])
        rstd = a.sb("rstd", [P, TILES])
        tmp = a.sb("tmp", [P, TILES])
        ss = a.sb("ss", [P, TILES])
        bank = [a.ps(f"t{b}", [P, 4, P]) for b in range(4)]
        loaded, summed, squared, meaned, rooted = (a.sem(s) for s in ("loaded", "summed", "squared", "meaned", "rooted"))
        normed, turned, weighted, hi_done, lo_done = (a.sem(s) for s in ("normed", "turned", "weighted", "hi_done", "lo_done"))
        stored, row_ready, dstep = (a.sem(s) for s in ("stored", "row_ready", "dstep"))
        loads = 2 + (norm is not None) + (add is not None) + (row is not None)
        hw = junk[:].rearrange("p (b k t) -> p b k t", b=4, k=4) if norm is not None else None
        block = ctx.enter_context(nc.Block())

        @block.sync
        def _(sp):
            sp.dma_start(X[:], src.rearrange("(t p) d -> p t d", p=P)).then_inc(loaded, 16)
            sp.dma_start(ident[:], ident_dram).then_inc(loaded, 16)
            if add is not None:
                sp.dma_start(Y[:], add.rearrange("(t p) d -> p t d", p=P)).then_inc(loaded, 16)
            if norm is not None:
                sp.dma_start(wcol[:], norm).then_inc(loaded, 16)
            stores = 0
            if add is not None:
                sp.wait_ge(summed, TILES)
                sp.dma_start(sum_dst.rearrange("(t p) d -> p t d", p=P), X[:]).then_inc(stored, 16)
                stores += 1
            if row is not None:
                sp.dma_start(Y[:, 1, :], row[0].partition_broadcast(P)).then_inc(loaded, 16)
                sp.wait_ge(row_ready, 1)
                sp.dma_start(row[1], Y[:, 2, :]).then_inc(stored, 16)
                stores += 1
            if spill is not None:
                sp.wait_ge(hi_done, 4 * TILES)
                sp.dma_start(spill[0], hi[:].bitcast(F32)).then_inc(stored, 16)
                sp.wait_ge(lo_done, 4 * TILES)
                sp.dma_start(spill[1], lo[:].bitcast(F32)).then_inc(stored, 16)
                stores += 2
            if stores:
                sp.wait_ge(stored, 16 * stores)

        @block.scalar
        def _(act):
            if norm is not None:
                if add is None:
                    act.wait_ge(loaded, 16 * loads)

            def tile(t):
                if norm is not None:
                    if add is not None:
                        act.wait_ge(summed, TILES)
                    wait(act, lo_done, 4 * t)
                    nc.scalar.activation(junk[:], X[:, bass.ds(t, 1), :].rearrange("p a d -> p (a d)"), ACT.Square,
                                         accum_out=ss[:, bass.ds(t, 1)]).then_inc(squared, 1)
                    act.wait_ge(meaned, t + 1)
                    nc.scalar.activation(root[:, bass.ds(t, 1)], mean[:, bass.ds(t, 1)], ACT.Sqrt).then_inc(rooted, 1)
                for b in range(4):
                    act.wait_ge(weighted if norm is not None else turned, 4 * t + b + 1)
                    part = hw[:, b, :, :] if norm is not None else bank[b][:]
                    nc.scalar.copy(hi[:, 4 * b:4 * b + 4, bass.ds(t * P, P)], part).then_inc(hi_done, 1)

            tile(0)
            with act.Fori(1, TILES) as t:
                tile(t)

        @block.vector
        def _(vec):
            dve = Steps(vec, dstep)
            vec.wait_ge(loaded, 16 * (loads - (row is not None)))
            if add is not None:
                with vec.Fori(0, TILES) as t:
                    nc.vector.tensor_tensor(X[:, bass.ds(t, 1), :], X[:, bass.ds(t, 1), :], Y[:, bass.ds(t, 1), :],
                                            ALU.add).then_inc(summed, 1)
                vec.wait_ge(summed, TILES)
            per = 6 if norm is not None else 0

            def tile(t):
                dve.at(t * per)
                at = bass.ds(t, 1)
                x = X[:, at, :].rearrange("p a d -> p (a d)")
                if norm is not None:
                    vec.wait_ge(squared, t + 1)
                    nc.vector.tensor_scalar(mean[:, at], ss[:, at], 1.0 / D, EPS, ALU.mult, ALU.add).then_inc(meaned, 1)
                    vec.wait_ge(meaned, t + 1)
                    vec.wait_ge(rooted, t + 1)
                    newton_rsqrt(nc, dve, rstd[:, at], mean[:, at], root[:, at], tmp[:, at])
                    dve(nc.vector.tensor_scalar(tmp[:, 0:1], rstd[:, at], 1.0, None, ALU.mult))
                    dve.wait()
                    wait(vec, turned, 4 * t)
                    nc.vector.tensor_scalar(xn[:], x, tmp[:, 0:1], None, ALU.mult).then_inc(normed, 1)
                    for b in range(4):
                        vec.wait_ge(turned, 4 * t + b + 1)
                        nc.vector.tensor_tensor(hw[:, b, :, :], bank[b][:], bcast(wcol[:, 4 * b:4 * b + 4], 2, P),
                                                ALU.mult).then_inc(weighted, 1)
                else:
                    wait(vec, turned, 4 * t)
                    nc.vector.tensor_scalar(xn[:], x, 1.0, None, ALU.mult).then_inc(normed, 1)
                for b in range(4):
                    if norm is not None:
                        vec.wait_ge(weighted, 4 * t + b + 1)
                    vec.wait_ge(hi_done, 4 * t + b + 1)
                    part = hw[:, b, :, :] if norm is not None else bank[b][:]
                    tok = bass.ds(t * P, P)
                    nc.vector.tensor_tensor(lo[:, 4 * b:4 * b + 4, tok], part, hi[:, 4 * b:4 * b + 4, tok].bitcast(F32),
                                            ALU.subtract).then_inc(lo_done, 1)

            tile(0)
            with vec.Fori(1, TILES) as t:
                tile(t)
            if row is not None:
                vec.wait_ge(loaded, 16 * loads)
                nc.vector.scalar_tensor_tensor(Y[:, 2, :], X[:, 0, :], rstd[:, 0:1], Y[:, 1, :], ALU.mult,
                                               ALU.mult).then_inc(row_ready, 1)

        @block.tensor
        def _(pe):
            pe.wait_ge(loaded, 16 * (loads - (row is not None)))

            def tile(t):
                pe.wait_ge(normed, t + 1)
                for b in range(4):
                    wait(pe, lo_done, 4 * (t - 1) + b + 1)
                    for k in range(4):
                        last = nc.tensor.transpose(bank[b][:, k, :], xn[:, (4 * b + k) * P:(4 * b + k + 1) * P], ident[:])
                    last.then_inc(turned, 1)

            tile(0)
            with pe.Fori(1, TILES) as t:
                tile(t)


def stream_matmul(nc, name, hi, lo, weights, dst, small=None):
    blocks, ks, halves, ht = weights.shape[0], KT // KQ, 2, TP // 2
    with ExitStack() as ctx:
        a = Alloc(nc, ctx, name)
        raw = [a.sb(f"raw{s}", [P, ks, NB]) for s in range(KQ)]
        whi = [a.sb(f"whi{s}", [P, ks, NB], F32R) for s in range(KQ)]
        wlo = [a.sb(f"wlo{s}", [P, ks, NB], F32R) for s in range(KQ)]
        stage = [a.sb(f"stage{t}", [P, NB]) for t in range(TILES)]
        acc = [a.ps(f"acc{t}", [P, NB]) for t in range(TILES)]
        raw_in = [a.sem(f"raw_in{s}") for s in range(KQ)]
        stored = [a.sem(f"stored{t}") for t in range(TILES)]
        hi_done, lo_done, unit_done, bank_done, staged = (
            a.sem(s) for s in ("hi_done", "lo_done", "unit_done", "bank_done", "staged"))
        if small is not None:
            half = [a.ps(f"half{s}", [P, ht]) for s in range(halves)]
            sstage = a.sb("sstage", [RANK, TP])
            small_in, small_hi, small_lo, small_done, small_staged, small_stored = (
                a.sem(f"small_{s}") for s in ("in", "hi", "lo", "done", "staged", "stored"))
        block = ctx.enter_context(nc.Block())

        @block.sync
        def _(sp):
            if small is not None:
                sp.dma_start(raw[0][:].rearrange("p a b -> p (a b)"),
                             small[0].rearrange("p k n -> p (k n)")).then_inc(small_in, 16)
                sp.wait_ge(small_lo, 1)

            def load(blk, q):
                wait(sp, lo_done, KQ * (blk - 1) + q + 1)
                sp.dma_start(raw[q][:], weights[blk, q]).then_inc(raw_in[q], 16)

            for q in range(KQ):
                load(0, q)
            with sp.Fori(1, blocks) as blk:
                for q in range(KQ):
                    load(blk, q)

        @block.scalar
        def _(act):
            def split_hi(blk, q):
                act.wait_ge(raw_in[q], 16 * (blk + 1))
                if q < KQ - 1:
                    wait(act, unit_done, (KQ - 1) * (blk - 1) + q + 1)
                else:
                    wait(act, bank_done, TILES * blk)
                nc.scalar.copy(whi[q][:], raw[q][:]).then_inc(hi_done, 1)

            def evacuate(blk):
                for t in range(TILES):
                    act.wait_ge(bank_done, TILES * blk + t + 1)
                    wait(act, stored[t], 16 * blk)
                    nc.scalar.copy(stage[t][:], acc[t][:]).then_inc(staged, 1)
                    act.wait_ge(staged, TILES * blk + t + 1)
                    act.dma_start(dst[t * P:(t + 1) * P, bass.ds(blk * NB, NB)], stage[t][:]).then_inc(stored[t], 16)

            if small is not None:
                act.wait_ge(small_in, 16)
                nc.scalar.copy(whi[0][:], raw[0][:]).then_inc(small_hi, 1)
                act.wait_ge(small_done, 1)
                for s in range(halves):
                    nc.scalar.copy(sstage[:, s * ht:(s + 1) * ht], half[s][0:RANK, :]).then_inc(small_staged, 1)
                act.wait_ge(small_staged, halves)
                act.dma_start(small[1], sstage[:]).then_inc(small_stored, 16)
            for q in range(KQ):
                split_hi(0, q)
            split_hi(1, 0)
            evacuate(0)
            with act.Fori(1, blocks - 1) as blk:
                for q in range(1, KQ):
                    split_hi(blk, q)
                split_hi(blk + 1, 0)
                evacuate(blk)
            for q in range(1, KQ):
                split_hi(blocks - 1, q)
            evacuate(blocks - 1)
            for t in range(TILES):
                act.wait_ge(stored[t], 16 * blocks)
            if small is not None:
                act.wait_ge(small_stored, 16)

        @block.vector
        def _(vec):
            if small is not None:
                vec.wait_ge(small_hi, 1)
                nc.vector.tensor_tensor(wlo[0][:], raw[0][:], whi[0][:].bitcast(F32), ALU.subtract).then_inc(small_lo, 1)
            with vec.Fori(0, blocks) as blk:
                for q in range(KQ):
                    vec.wait_ge(hi_done, KQ * blk + q + 1)
                    nc.vector.tensor_tensor(wlo[q][:], raw[q][:], whi[q][:].bitcast(F32),
                                            ALU.subtract).then_inc(lo_done, 1)

        @block.tensor
        def _(pe):
            if small is not None:
                pe.wait_ge(small_lo, 1)
                for s in range(halves):
                    tok = slice(s * ht, (s + 1) * ht)
                    for k in range(KT):
                        w = [x[:].rearrange("p a (b n) -> p (a b) n", n=P)[:, k, :] for x in (whi[0], wlo[0])]
                        nc.tensor.matmul(half[s][:], w[0], hi[:, k, tok], start=k == 0, stop=False)
                        nc.tensor.matmul(half[s][:], w[0], lo[:, k, tok], start=False, stop=False)
                        last = nc.tensor.matmul(half[s][:], w[1], hi[:, k, tok], start=False, stop=k == KT - 1)
                last.then_inc(small_done, 1)

            def products(blk):
                for q in range(KQ):
                    pe.wait_ge(lo_done, KQ * blk + q + 1)
                    for t in range(TILES):
                        if q == 0:
                            wait(pe, staged, TILES * (blk - 1) + t + 1)
                        tok = slice(t * P, (t + 1) * P)
                        for k in range(ks):
                            kk = q * ks + k
                            first, end = kk == 0, kk == KT - 1
                            nc.tensor.matmul(acc[t][:], hi[:, kk, tok], whi[q][:, k, :], start=first, stop=False)
                            nc.tensor.matmul(acc[t][:], hi[:, kk, tok], wlo[q][:, k, :], start=False, stop=False)
                            last = nc.tensor.matmul(acc[t][:], lo[:, kk, tok], whi[q][:, k, :], start=False, stop=end)
                        if q == KQ - 1:
                            last.then_inc(bank_done, 1)
                    if q < KQ - 1:
                        last.then_inc(unit_done, 1)

            products(0)
            with pe.Fori(1, blocks) as blk:
                products(blk)


def mixer(nc, name, c, proj, alr_dram, w_a2, gn, states, new_states, mix):
    W = 4 * P
    with ExitStack() as ctx:
        a = Alloc(nc, ctx, name)
        qk_r = a.sb("qk_r", [P, 8, DK])
        v_r = a.sb("v_r", [P, H, DV])
        g_r = a.sb("g_r", [P, H * DV])
        qk_g = a.sb("qk_g", [P, 8, DK])
        v_g = a.sb("v_g", [P, H, DV])
        g_g = a.sb("g_g", [P, H * DV])
        parts = [(qk_r, QR), (v_r, VR), (g_r, GR), (qk_g, QG), (v_g, VG), (g_g, GG)]
        ident = a.sb("ident", [P, P])
        rope = a.sb("rope", [P, TILES, 2, DK // 2])
        mask_r = a.sb("mask_r", [P, H, P])
        mask_rs = a.sb("mask_rs", [NSMP, H, NSMP])
        qdec = a.sb("qdec", [P, H, P])
        qdec_s = a.sb("qdec_s", [P, H, NSMP])
        kdec = a.sb("kdec", [P, H])
        kdec_s = a.sb("kdec_s", [NSMP, H])
        causal = a.sb("causal", [P, P])
        causal_s = a.sb("causal_s", [NSMP, NSMP])
        keep = a.sb("keep", [P, W])
        keep_s = a.sb("keep_s", [P, H * NSMP])
        seq_cols = a.sb("seq_cols", [P, NSEQ, NSMP])
        seq_rows = a.sb("seq_rows", [NSMP, NSEQ])
        gnb = a.sb("gnb", [P, 3, H * DV])
        wa2 = a.sb("wa2", [RANK + 1, H * DK])
        alr = a.sb("alr", [RANK + 1, TP])
        consts = [(ident, c["ident"]), (rope, c["rope"]), (mask_r, c["mask_r"]), (mask_rs, c["mask_rs"]),
                  (qdec, c["qdec"]), (qdec_s, c["qdec_s"]), (kdec, c["kdec"]), (kdec_s, c["kdec_s"]),
                  (causal, c["causal"]), (causal_s, c["causal_s"]), (keep, c["keep"]), (keep_s, c["keep_s"]),
                  (seq_cols, c["seq_cols"]), (seq_rows, c["seq_rows"]), (wa2, w_a2)]

        rot = a.sb("rot", [P, 8, DK])
        ra = a.sb("ra", [P, 8, DK // 2])
        rb = a.sb("rb", [P, 8, DK // 2])
        kd = a.sb("kd", [P, H, DK])
        qT = a.sb("qT", [P, H, P])
        kT = a.sb("kT", [P, H, P])
        qdT = a.sb("qdT", [P, H, P])
        at_r = a.sb("at_r", [P, H, P])
        at_g = a.sb("at_g", [P, H, P])
        at_gs = a.sb("at_gs", [NSMP, H, NSMP])
        S_r = a.sb("S_r", [P, H, DV])
        S_g = a.sb("S_g", [P, H, DV])
        stats = a.sb("stats", [P, H, 6])
        mv = a.sb("mv", [P, H, 2])
        var = a.sb("var", [P, H])
        root = a.sb("root", [P, H])
        rstd = a.sb("rstd", [P, H])
        tmp = a.sb("tmp", [P, H])
        silu = a.sb("silu", [P, H * DV])
        out = a.sb("out", [P, 2, H * DV])
        z_abs = a.sb("z_abs", [P, W])
        cum = a.sb("cum", [P, W])
        lna = a.sb("lna", [P, W])
        ND_, NO = 4 * 4 * 4 * BLK, H * (BLK + 2 * BLK + 3 * BLK)
        dec = a.sb("dec", [P, ND_ + NO + W + 3 * H * BLK + W + W])
        klr = a.sb("klr", [P, H, DK])
        sdec = a.sb("sdec", [P, H, NSEQ])
        S8 = [a.sb(f"S8_{s}", [P, NSEQ, DV]) for s in range(2)]
        qm = a.sb("qm", [P, NSEQ, NSMP])
        km = a.sb("km", [NSMP, NSEQ, DK])

        tr = [a.ps(f"tr{b}", [P, 4, P]) for b in range(2)]
        sc = a.ps("sc", [P, 4 * P])
        op = [a.ps(f"o{b}", [P, 2, DV]) for b in range(2)]
        st = [a.ps(f"st{b}", [P, 2, DV]) for b in range(2)]
        zp = a.ps("z", [P, W])

        part_in = [a.sem(f"part_in{n}") for n in range(6)]
        const_in, alr_in, ones_set, zeros_set = (a.sem(s) for s in ("const_in", "alr_in", "ones_set", "zeros_set"))
        (rotated, k_decayed, r_turned, r_copied, q_decayed, r_scored, r_masked, r_out, r_states, r_stepped,
         r_var, r_root, r_silu, r_mixed) = (a.sem(s) for s in (
             "rotated", "k_decayed", "r_turned", "r_copied", "q_decayed", "r_scored", "r_masked", "r_out", "r_states",
             "r_stepped", "r_var", "r_root", "r_silu", "r_mixed"))
        (z_made, z_log, args_made, decays_made, g_turned, g_weighted, g_scored, g_masked, g_out, kl_turned, kl_copied,
         g_states, g_stepped, g_squared, g_var, g_root, g_silu, g_mixed) = (a.sem(s) for s in (
             "z_made", "z_log", "args_made", "decays_made", "g_turned", "g_weighted", "g_scored", "g_masked", "g_out",
             "kl_turned", "kl_copied", "g_states", "g_stepped", "g_squared", "g_var", "g_root", "g_silu", "g_mixed"))
        r_mix_stored, g_mix_stored = a.gpsimd_dma_sem("r_mix_stored"), a.gpsimd_dma_sem("g_mix_stored")
        s8_in = [a.gpsimd_dma_sem(f"s8_in{s}") for s in range(2)]
        s8_out = [a.gpsimd_dma_sem(f"s8_out{s}") for s in range(2)]
        q_masked, k_masked, seq_states, seq_stepped = (a.sem(s) for s in ("q_masked", "k_masked", "seq_states", "seq_stepped"))
        final_out, dstep, astep = a.sem("final_out"), a.sem("dstep"), a.sem("astep")
        block = ctx.enter_context(nc.Block())

        def rows(t):
            return P if not (isinstance(t, int) and t == PTILES) else NSMP

        def seg(t, kind):
            R = rows(t)
            G = R // BLK
            size = {"D": H * G * 4 * BLK, "O1": H * BLK, "O2": 2 * H * BLK, "O3": 3 * H * BLK,
                    "Q8": H * R, "QO": 3 * H * BLK, "QC": H * R, "KL": H * R}
            at = 0
            for k, n in size.items():
                if R == NSMP and k in ("O1", "O2", "O3", "QO"):
                    continue
                if k == kind:
                    return dec[:, at:at + n]
                at += n
            return at

        n_consts = len(consts) + 3

        @block.sync
        def _(sp):
            for tile_, src in consts:
                sp.dma_start(tile_[:], src).then_inc(const_in, 16)
            for n in range(3):
                sp.dma_start(gnb[:, n, :], gn[n].partition_broadcast(P)).then_inc(const_in, 16)
            sp.wait_ge(ones_set, 1)
            sp.dma_start(alr[0:RANK, :], alr_dram).then_inc(alr_in, 16)

            def load(t, n, used, count):
                if not (isinstance(t, int) and t == 0):
                    sp.wait_ge(used, count)
                R = rows(t)
                buf, col = parts[n]
                flat = buf[:].rearrange("p a b -> p (a b)") if len(buf.shape) == 3 else buf[:]
                sp.dma_start(flat[0:R, :], proj[bass.ds(t * P, R), col:col + 1024]).then_inc(part_in[n], 16)

            def tile(t):
                load(t, 0, rotated, 2 * t)
                load(t, 1, r_states, t)
                load(t, 2, r_silu, t)
                load(t, 3, g_turned, t)
                load(t, 4, g_states, t)
                load(t, 5, g_silu, t)

            tile(0)
            with sp.Fori(1, PTILES) as t:
                tile(t)
            tile(PTILES)
            for n in range(2):
                S = (S_r, S_g)[n]
                sp.wait_ge((r_stepped, g_stepped)[n], PTILES)
                sp.dma_start(new_states[0][n].rearrange("h d v -> d h v"), S[:]).then_inc(final_out, 16)
            sp.wait_ge(final_out, 32)

        @block.gpsimd
        def _(pool):
            def move_in(n):
                s, group, h = n % 2, n // H, n % H
                wait(pool, s8_out[s], 16 * (n // 2))
                pool.dma_start(S8[s][:], states[group][:, h].rearrange("b d v -> d b v")).then_inc(s8_in[s], 16)

            def store_mix(t, group):
                pool.wait_ge((r_mixed, g_mixed)[group], t + 1)
                pool.dma_start(mix[bass.ds(t * P, P), group * 1024:(group + 1) * 1024], out[:, group, :]).then_inc(
                    (r_mix_stored, g_mix_stored)[group], 16)

            move_in(0)
            move_in(1)
            with pool.Fori(0, PTILES) as t:
                store_mix(t, 0)
                store_mix(t, 1)
            for n in range(2 * H):
                s, group, h = n % 2, n // H, n % H
                pool.wait_ge(seq_stepped, 4 * (n + 1))
                pool.dma_start(new_states[1][group][:, h].rearrange("b d v -> d b v"), S8[s][:]).then_inc(s8_out[s], 16)
                if n + 2 < 2 * H:
                    move_in(n + 2)
                if n % H == H - 1:
                    store_mix(PTILES, group)
            for s in range(2):
                pool.wait_ge(s8_out[s], 16 * H)
            pool.wait_ge(r_mix_stored, 16 * TILES)
            pool.wait_ge(g_mix_stored, 16 * TILES)

        @block.scalar
        def _(act):
            step = Steps(act, astep)
            act.wait_ge(const_in, 16 * n_consts)

            def tile(t):
                R = rows(t)
                step.at(5 * t)
                cols = slice(0, R)
                act.wait_ge(r_turned, t + 1)
                wait(act, r_scored, t)
                nc.scalar.copy(qT[:, :, cols], tr[0][:, :, cols]).then_inc(r_copied, 1)
                nc.scalar.copy(kT[:, :, cols], tr[1][:, :, cols]).then_inc(r_copied, 1)
                act.wait_ge(z_made, t + 1)
                wait(act, z_log, t)
                zl, zr = z_abs[:, 0:H * R], zp[:, 0:H * R]
                step(nc.scalar.activation(zl, zr, ACT.Abs))
                step.wait()
                step(nc.scalar.activation(zl, zl, ACT.Exp, scale=-1.0))
                step.wait()
                nc.scalar.activation(zl, zl, ACT.Ln, bias=1.0).then_inc(z_log, 1)
                act.wait_ge(args_made, t + 1)
                n = seg(t, None)
                nc.scalar.activation(dec[:, 0:n], dec[:, 0:n], ACT.Exp).then_inc(decays_made, 1)
                act.wait_ge(r_var, t + 1)
                nc.scalar.activation(root[0:R, :], var[0:R, :], ACT.Sqrt).then_inc(r_root, 1)
                act.wait_ge(part_in[2], 16 * (t + 1))
                wait(act, g_mixed, t)
                nc.scalar.activation(silu[0:R, :], g_r[0:R, :], ACT.Silu).then_inc(r_silu, 1)
                act.wait_ge(kl_turned, t + 1)
                nc.scalar.copy(klr[0:R, :, :], tr[0][0:R, :, :]).then_inc(kl_copied, 1)
                act.wait_ge(g_out, t + 1)
                act.wait_ge(decays_made, t + 1)
                for h in range(H):
                    ins = nc.scalar.activation(z_abs[0:R, 0:DV], op[h // 2][0:R, h % 2, :], ACT.Square,
                                               accum_out=mv[0:R, h, 0:1])
                    if h < H - 1:
                        step(ins)
                        step.wait()
                ins.then_inc(g_squared, 1)
                act.wait_ge(g_var, t + 1)
                nc.scalar.activation(root[0:R, :], var[0:R, :], ACT.Sqrt).then_inc(g_root, 1)
                act.wait_ge(part_in[5], 16 * (t + 1))
                act.wait_ge(r_mixed, t + 1)
                nc.scalar.activation(silu[0:R, :], g_g[0:R, :], ACT.Silu).then_inc(g_silu, 1)

            tile(0)
            with act.Fori(1, PTILES) as t:
                tile(t)
            tile(PTILES)

        @block.vector
        def _(vec):
            d = Steps(vec, dstep)
            tt, mult = nc.vector.tensor_tensor, ALU.mult
            nc.vector.memset(alr[:], 1.0).then_inc(ones_set, 1)
            for z in (S_r, S_g, at_g, at_gs):
                nc.vector.memset(z[:], 0.0).then_inc(zeros_set, 1)
            vec.wait_ge(zeros_set, 4)
            vec.wait_ge(const_in, 16 * n_consts)

            def finish_group(t, group, weight):
                R = rows(t)
                o = out[0:R, group, :]
                d(tt(o, o, gnb[0:R, weight, :], mult))
                d.wait()
                if group == 0:
                    d(tt(o, o, gnb[0:R, 1, :], ALU.add))
                    d.wait()
                vec.wait_ge((r_silu, g_silu)[group], t + 1)
                tt(o, o, silu[0:R, :], mult).then_inc((r_mixed, g_mixed)[group], 1)

            def sample_head(n, group, h, qsrc, ksrc):
                s = n % 2
                vec.wait_ge((q_decayed, g_weighted)[group], PTILES + 1)
                vec.wait_ge(k_decayed, PTILES + 1)
                wait(vec, seq_states, 2 * n)
                tt(qm[:], bcast(qsrc, 1, NSEQ), seq_cols[:], mult).then_inc(q_masked, 1)
                tt(km[:], bcast(ksrc, 1, NSEQ), bcast(seq_rows[:], 2, DK), mult).then_inc(k_masked, 1)
                for half in range(2):
                    vec.wait_ge(seq_states, 2 * n + half + 1)
                    if half == 0:
                        vec.wait_ge(s8_in[s], 16 * (n // 2 + 1))
                    for pair in range(2):
                        b = 4 * half + 2 * pair
                        S = S8[s][:, b:b + 2, :]
                        if group == 0:
                            nc.vector.scalar_tensor_tensor(S, S, GAMMA[h] ** LSEQ, st[pair][:], mult,
                                                           ALU.add).then_inc(seq_stepped, 1)
                        else:
                            for x in range(2):
                                ins = nc.vector.scalar_tensor_tensor(S[:, x, :], S[:, x, :], sdec[:, h, b + x:b + x + 1],
                                                                     st[pair][:, x, :], mult, ALU.add)
                                if x == 0:
                                    d(ins)
                            ins.then_inc(seq_stepped, 1)

            def tile(t):
                R = rows(t)
                smp = R == NSMP
                G = R // BLK
                cols = slice(0, R)
                d.at(per_tile[0] * t)
                vec.wait_ge(part_in[0], 16 * (t + 1))
                cos = bcast(rope[0:R, bass.ds(t, 1), 0, :].rearrange("p a f -> p (a f)"), 1, 8)
                sin = bcast(rope[0:R, bass.ds(t, 1), 1, :].rearrange("p a f -> p (a f)"), 1, 8)
                x1, x2 = qk_r[0:R, :, 0:64], qk_r[0:R, :, 64:128]
                wait(vec, r_turned, t)
                wait(vec, k_decayed, t)
                d(tt(ra[0:R], x1, cos, mult))
                d(tt(rb[0:R], x2, sin, mult))
                d.wait()
                tt(rot[0:R, :, 0:64], ra[0:R], rb[0:R], ALU.subtract).then_inc(rotated, 1)
                vec.wait_ge(rotated, 2 * t + 1)
                d(tt(ra[0:R], x1, sin, mult))
                d(tt(rb[0:R], x2, cos, mult))
                d.wait()
                tt(rot[0:R, :, 64:128], ra[0:R], rb[0:R], ALU.add).then_inc(rotated, 1)
                vec.wait_ge(rotated, 2 * t + 2)
                wait(vec, r_states, t)
                tt(kd[0:R], rot[0:R, 4:8, :], bcast((kdec_s if smp else kdec)[:], 2, DK), mult).then_inc(k_decayed, 1)
                vec.wait_ge(r_copied, 2 * t + 1)
                wait(vec, r_out, t)
                tt(qdT[:, :, cols], tr[0][:, :, cols], (qdec_s if smp else qdec)[:], mult).then_inc(q_decayed, 1)
                vec.wait_ge(z_log, t + 1)
                zl, zr, la, cu = z_abs[:, 0:H * R], zp[:, 0:H * R], lna[:, 0:H * R], cum[:, 0:H * R]
                d(nc.vector.scalar_tensor_tensor(la, zr, 0.0, zl, ALU.min, ALU.subtract))
                d.wait()
                d(nc.vector.tensor_scalar(la, la, 1.0 / TEMP, LOG_A_MIN, mult, ALU.max))
                d.wait()
                d(nc.vector.tensor_tensor_scan(cu, (keep_s if smp else keep)[:], la, 0.0, mult, ALU.add))
                d.wait()
                vec.wait_ge(r_scored, t + 1)
                wait(vec, r_out, t)
                scv = sc[0:R, 0:H * R].rearrange("p (h i) -> p h i", h=H)
                tt(at_r[0:R, :, cols], scv, (mask_rs if smp else mask_r)[:], mult).then_inc(r_masked, 1)
                wait(vec, g_out, t)
                wait(vec, kl_turned, t)
                sub = ALU.subtract
                c3 = cu.rearrange("p (h i) -> p h i", h=H)
                ref8 = cu.rearrange("p (s i) -> p s i", i=SUB)[:, :, SUB // 2 - 1]
                D = seg(t, "D").rearrange("p (b s j) -> p b s j", s=4, j=BLK)
                d(tt(D, bcast(ref8.rearrange("p (b s) -> p b s", s=4), 3, BLK),
                     bcast(cu.rearrange("p (b j) -> p b j", j=BLK), 2, 4), sub))
                d(tt(seg(t, "Q8").rearrange("p (s i) -> p s i", i=SUB), cu.rearrange("p (s i) -> p s i", i=SUB),
                     bcast(ref8, 2, SUB), sub))
                if not smp:
                    for g in (1, 2, 3):
                        ref = c3[:, :, BLK * g - 1]
                        O = seg(t, f"O{g}").rearrange("p (h j) -> p h j", h=H)
                        d(tt(O, bcast(ref, 2, BLK * g), c3[:, :, 0:BLK * g], sub))
                    refs = cu.rearrange("p (h g i) -> p h g i", h=H, i=BLK)
                    d(tt(seg(t, "QO").rearrange("p (h g i) -> p h g i", h=H, i=BLK), refs[:, :, 1:4, :],
                         bcast(refs[:, :, 0:3, BLK - 1], 3, BLK), sub))
                    last = bcast(c3[:, :, R - 1], 2, R)
                    d(tt(seg(t, "KL").rearrange("p (h i) -> p h i", h=H), last, c3, sub))
                else:
                    seqs = cu.rearrange("p (s i) -> p s i", i=LSEQ)
                    d(tt(seg(t, "KL").rearrange("p (s i) -> p s i", i=LSEQ), bcast(seqs[:, :, LSEQ - 1], 2, LSEQ), seqs, sub))
                d(nc.vector.tensor_scalar(seg(t, "QC"), cu, 1.0, None, mult))
                d.wait()
                Df = seg(t, "D")
                nc.vector.tensor_scalar(Df, Df, EXP_MAX, None, ALU.min).then_inc(args_made, 1)
                if not smp:
                    vec.wait_ge(r_states, t + 1)
                    for h in range(H):
                        ins = nc.vector.scalar_tensor_tensor(S_r[:, h, :], S_r[:, h, :], GAMMA[h] ** P, st[h // 2][:, h % 2, :],
                                                             mult, ALU.add)
                        if h < H - 1:
                            d(ins)
                    ins.then_inc(r_stepped, 1)
                else:
                    for h in range(H):
                        sample_head(h, 0, h, qdT[:, h, cols], kd[0:R, h, :])
                vec.wait_ge(r_out, t + 1)
                for h in range(H):
                    d(nc.vector.bn_stats(stats[0:R, h, :], op[h // 2][0:R, h % 2, :]))
                d.wait()
                ev, od = stats[0:R, :, 0:3], stats[0:R, :, 3:6]
                d(tt(mv[0:R, :, 0], ev[:, :, 1], od[:, :, 1], ALU.add))
                d(tt(mv[0:R, :, 1], ev[:, :, 1], od[:, :, 1], ALU.subtract))
                d(tt(var[0:R, :], ev[:, :, 2], od[:, :, 2], ALU.add))
                d.wait()
                d(nc.vector.tensor_scalar(mv[0:R, :, 0], mv[0:R, :, 0], 0.5, None, mult))
                d(nc.vector.scalar_tensor_tensor(tmp[0:R, :], mv[0:R, :, 1], 0.25, mv[0:R, :, 1], mult, mult))
                d(nc.vector.tensor_scalar(var[0:R, :], var[0:R, :], 1.0 / DV, EPS, mult, ALU.add))
                d.wait()
                tt(var[0:R, :], var[0:R, :], tmp[0:R, :], ALU.add).then_inc(r_var, 1)
                vec.wait_ge(r_var, t + 1)
                vec.wait_ge(r_root, t + 1)
                newton_rsqrt(nc, d, rstd[0:R], var[0:R], root[0:R], tmp[0:R])
                wait(vec, r_mix_stored, 16 * t)
                for h in range(H):
                    d(nc.vector.tensor_scalar(out[0:R, 0, h * DV:(h + 1) * DV], op[h // 2][0:R, h % 2, :], mv[0:R, h, 0:1],
                                              rstd[0:R, h:h + 1], sub, mult))
                d.wait()
                finish_group(t, 0, 0)
                vec.wait_ge(decays_made, t + 1)
                vec.wait_ge(g_turned, t + 1)
                qs, ks = tr[0][:, :, cols], tr[1][:, :, cols]
                h3 = lambda x: x.rearrange("p (h i) -> p h i", h=H)
                stt, scale = nc.vector.scalar_tensor_tensor, DK ** -0.5
                if smp:
                    d(nc.vector.tensor_copy(sdec[:], seg(t, "QC").rearrange("p (h s i) -> p h s i", h=H, i=LSEQ)[:, :, :, LSEQ - 1]))
                else:
                    d(nc.vector.tensor_copy(sdec[:, :, 0], h3(seg(t, "QC"))[:, :, R - 1]))
                d.wait()
                for b in range(H):
                    Db = D[:, b * G:(b + 1) * G]
                    d(tt(Db, Db, bcast(ks[:, b, :].rearrange("p (g j) -> p g j", j=BLK), 2, 4), mult))
                d(stt(h3(seg(t, "Q8")), h3(seg(t, "Q8")), scale, qs, mult, mult))
                d(stt(h3(seg(t, "QC")), h3(seg(t, "QC")), scale, qs, mult, mult))
                if not smp:
                    for g in (1, 2, 3):
                        O = h3(seg(t, f"O{g}"))
                        d(tt(O, O, ks[:, :, 0:BLK * g], mult))
                    d(stt(h3(seg(t, "QO")), h3(seg(t, "QO")), scale, qs[:, :, BLK:R], mult, mult))
                tt(h3(seg(t, "KL")), h3(seg(t, "KL")), ks, mult).then_inc(g_weighted, 1)
                vec.wait_ge(g_scored, t + 1)
                dst, msk = (at_gs, causal_s) if smp else (at_g, causal)
                for g in range(G):
                    r = slice(BLK * g, BLK * (g + 1))
                    cc = slice(BLK * g, BLK * (g + 1) if smp else R)
                    n = cc.stop - cc.start
                    ins = tt(dst[r, :, cc], scv[r, :, cc], bcast(msk[r, cc], 1, H), mult)
                    if g < G - 1:
                        d(ins)
                ins.then_inc(g_masked, 1)
                if smp:
                    vec.wait_ge(kl_copied, t + 1)
                    for h in range(H):
                        sample_head(H + h, 1, h, h3(seg(t, "QC"))[:, h, :], klr[0:R, h, :])
                vec.wait_ge(g_squared, t + 1)
                nc.vector.tensor_scalar(var[0:R, :], mv[0:R, :, 0], 1.0 / DV, EPS, mult, ALU.add).then_inc(g_var, 1)
                vec.wait_ge(g_var, t + 1)
                vec.wait_ge(g_root, t + 1)
                newton_rsqrt(nc, d, rstd[0:R], var[0:R], root[0:R], tmp[0:R])
                wait(vec, g_mix_stored, 16 * t)
                for h in range(H):
                    d(nc.vector.tensor_scalar(out[0:R, 1, h * DV:(h + 1) * DV], op[h // 2][0:R, h % 2, :],
                                              rstd[0:R, h:h + 1], None, mult))
                d.wait()
                finish_group(t, 1, 2)
                if not smp:
                    vec.wait_ge(g_states, t + 1)
                    for h in range(H):
                        ins = stt(S_g[:, h, :], S_g[:, h, :], sdec[:, h, 0:1], st[h // 2][:, h % 2, :], mult, ALU.add)
                        if h < H - 1:
                            d(ins)
                    ins.then_inc(g_stepped, 1)

            per_tile = [0]
            tile(0)
            per_tile[0] = d.n
            with vec.Fori(1, PTILES) as t:
                tile(t)
            tile(PTILES)

        @block.tensor
        def _(pe):
            mm = nc.tensor.matmul
            pe.wait_ge(const_in, 16 * n_consts)
            pe.wait_ge(alr_in, 16)
            pe.wait_ge(zeros_set, 4)

            def tile(t):
                R = rows(t)
                smp = R == NSMP
                G = R // BLK
                wait(pe, z_log, t)
                wait(pe, args_made, t)
                for h in range(H):
                    ins = mm(zp[:, h * R:(h + 1) * R], wa2[:, h * DK:(h + 1) * DK], alr[:, bass.ds(t * P, R)],
                             start=True, stop=True)
                ins.then_inc(z_made, 1)
                pe.wait_ge(rotated, 2 * t + 2)
                wait(pe, kl_copied, t)
                for n in range(8):
                    ins = nc.tensor.transpose(tr[n // 4][:, n % 4, 0:R], rot[0:R, n, :], ident[0:R, 0:R])
                ins.then_inc(r_turned, 1)
                pe.wait_ge(r_copied, 2 * t + 2)
                wait(pe, g_masked, t)
                for h in range(H):
                    ins = mm(sc[0:R, h * R:(h + 1) * R], kT[:, h, 0:R], qT[:, h, 0:R], start=True, stop=True)
                ins.then_inc(r_scored, 1)
                pe.wait_ge(q_decayed, t + 1)
                pe.wait_ge(part_in[3], 16 * (t + 1))
                for n in range(8):
                    ins = nc.tensor.transpose(tr[n // 4][:, n % 4, 0:R], qk_g[0:R, n, :], ident[0:R, 0:R])
                ins.then_inc(g_turned, 1)
                pe.wait_ge(r_masked, t + 1)
                pe.wait_ge(part_in[1], 16 * (t + 1))
                wait(pe, g_mixed, t)
                wait(pe, r_stepped, t)
                if not smp:
                    for h in range(H):
                        o = op[h // 2][0:R, h % 2, :]
                        mm(o, at_r[0:R, h, 0:R], v_r[0:R, h, :], start=True, stop=False)
                        ins = mm(o, qdT[:, h, 0:R], S_r[:, h, :], start=False, stop=True)
                    ins.then_inc(r_out, 1)
                    pe.wait_ge(k_decayed, t + 1)
                    wait(pe, g_stepped, t)
                    for h in range(H):
                        ins = mm(st[h // 2][:, h % 2, :], kd[0:R, h, :], v_r[0:R, h, :], start=True, stop=True)
                    ins.then_inc(r_states, 1)
                else:
                    pe.wait_ge(g_stepped, PTILES)
                    sample_heads(0, at_r, v_r, r_out)
                pe.wait_ge(g_weighted, t + 1)
                D = seg(t, "D").rearrange("p (h g s j) -> p h g s j", h=H, s=4, j=BLK)
                h3 = lambda x: x.rearrange("p (h i) -> p h i", h=H)
                for h in range(H):
                    for g in range(G):
                        for s in range(BLK // SUB):
                            i = BLK * g + SUB * s
                            ins = mm(sc[BLK * g:BLK * (g + 1), h * R + i:h * R + i + SUB], D[:, h, g, s, :],
                                     h3(seg(t, "Q8"))[:, h, i:i + SUB], start=True, stop=True)
                        if g > 0 and not smp:
                            ins = mm(sc[0:BLK * g, h * R + BLK * g:h * R + BLK * (g + 1)], h3(seg(t, f"O{g}"))[:, h, :],
                                     h3(seg(t, "QO"))[:, h, BLK * (g - 1):BLK * g], start=True, stop=True)
                ins.then_inc(g_scored, 1)
                for h in range(H):
                    ins = nc.tensor.transpose(tr[0][0:R, h, :], h3(seg(t, "KL"))[:, h, :], ident[:])
                ins.then_inc(kl_turned, 1)
                pe.wait_ge(g_masked, t + 1)
                pe.wait_ge(part_in[4], 16 * (t + 1))
                pe.wait_ge(r_mixed, t + 1)
                if not smp:
                    for h in range(H):
                        o = op[h // 2][0:R, h % 2, :]
                        mm(o, at_g[0:R, h, 0:R], v_g[0:R, h, :], start=True, stop=False)
                        ins = mm(o, h3(seg(t, "QC"))[:, h, :], S_g[:, h, :], start=False, stop=True)
                    ins.then_inc(g_out, 1)
                    pe.wait_ge(kl_copied, t + 1)
                    pe.wait_ge(r_stepped, t + 1)
                    for h in range(H):
                        ins = mm(st[h // 2][:, h % 2, :], klr[0:R, h, :], v_g[0:R, h, :], start=True, stop=True)
                    ins.then_inc(g_states, 1)
                else:
                    sample_heads(1, at_gs, v_g, g_out)

            def sample_heads(group, at, v, done):
                R = NSMP
                for h in range(H):
                    n = H * group + h
                    o = op[h // 2][0:R, h % 2, :]
                    mm(o, at[0:R, h, 0:R], v[0:R, h, :], start=True, stop=False)
                    pe.wait_ge(s8_in[n % 2], 16 * (n // 2 + 1))
                    pe.wait_ge(q_masked, n + 1)
                    for b in range(NSEQ):
                        ins = mm(o, qm[:, b, :], S8[n % 2][:, b, :], start=False, stop=b == NSEQ - 1)
                    if h == H - 1:
                        ins.then_inc(done, 1)
                    pe.wait_ge(k_masked, n + 1)
                    for half in range(2):
                        wait(pe, seq_stepped, 4 * n + 2 * half)
                        for b in range(4):
                            ins = mm(st[b // 2][:, b % 2, :], km[:, 4 * half + b, :], v[0:R, h, :], start=True, stop=True)
                        ins.then_inc(seq_states, 1)

            tile(0)
            with pe.Fori(1, PTILES) as t:
                tile(t)
            tile(PTILES)


def constants():
    f = np.float32
    pos = np.concatenate([np.arange(SEQ), np.tile(PAST + np.arange(LSEQ), NSEQ), np.zeros(TP - SEQ - NSMP)]).astype(f)
    freqs = (f(10000.0) ** (-np.arange(0, DK, 2, dtype=f) / f(DK))).astype(f)
    ang = (pos[:, None] * freqs[None, :]).astype(f)
    rope = np.stack([np.cos(ang.astype(np.float64)), np.sin(ang.astype(np.float64))], 1)
    rope = rope.reshape(TILES, P, 2, DK // 2).transpose(1, 0, 2, 3)
    lg = np.log1p(-np.exp2(-5.0 - np.arange(H)))
    scale = DK ** -0.5

    def masks(L, n):
        i = np.arange(L * n)
        dist = i[None, :] - i[:, None]
        ok = (dist >= 0) & (i[None, :] // L == i[:, None] // L)
        decay = np.where(ok[None], np.exp(np.maximum(dist, 0)[None] * lg[:, None, None]), 0.0) * scale
        q = np.exp((i % L + 1)[None, :] * lg[:, None])
        k = np.exp((L - 1 - i % L)[None, :] * lg[:, None]) * scale
        return (ok, decay.transpose(1, 0, 2), np.broadcast_to(q[None], (P, H, L * n)), k.T)

    ok, mask_r, qdec, kdec = masks(P, 1)
    ok_s, mask_rs, qdec_s, kdec_s = masks(LSEQ, NSEQ)
    keep = np.ones((P, H, P))
    keep[:, :, 0] = 0
    keep_s = np.ones((P, H * NSEQ, LSEQ))
    keep_s[:, :, 0] = 0
    seq = np.arange(NSMP)[None, :] // LSEQ == np.arange(NSEQ)[:, None]
    out = dict(ident=np.eye(P), rope=rope, mask_r=mask_r, mask_rs=mask_rs, qdec=qdec, qdec_s=qdec_s, kdec=kdec,
               kdec_s=kdec_s, causal=ok, causal_s=ok_s, keep=keep.reshape(P, -1), keep_s=keep_s.reshape(P, -1),
               seq_cols=np.broadcast_to(seq[None], (P, NSEQ, NSMP)), seq_rows=seq.T,
               iota=np.broadcast_to(np.arange(P)[None], (P, P)))
    return {k: np.ascontiguousarray(v, dtype=f) for k, v in out.items()}


def route(nc, name, c, queries, keys, expert_ids, gates0, firsts, seconds, gates):
    HS, C2 = 2 * HEADS, TOPK * TOPK
    with ExitStack() as ctx:
        a = Alloc(nc, ctx, name)
        q = a.sb("q", [P, HS * DQ])
        ident = a.sb("ident", [P, P])
        kt = a.sb("keys", [P, HS, NKEYS])
        qT = a.sb("qT", [P, HS, P])
        s = [a.sb(f"s{n}", [P, HS, NKEYS]) for n in range(2)]
        vals = a.sb("vals", [P, HS, TOPK])
        idx = a.sb("idx", [P, HS, TOPK], U32)
        idxf = a.sb("idxf", [P, HS, TOPK])
        cand = [a.sb(f"cand{n}", [P, HEADS, C2]) for n in range(2)]
        top = a.sb("top", [P, HEADS, TOPK])
        sel = a.sb("sel", [P, HEADS, TOPK], U32)
        half = [a.sb(f"half{n}", [P, HEADS, TOPK], U32) for n in range(2)]
        halff = [a.sb(f"halff{n}", [P, HEADS, TOPK]) for n in range(2)]
        iota = a.sb("iota", [P, TOPK])
        hot = [a.sb(f"hot{n}", [P, HK, TOPK]) for n in range(2)]
        picked = [a.sb(f"picked{n}", [P, HK]) for n in range(2)]
        gate = a.sb("gate", [P, HEADS, TOPK])
        total = a.sb("total", [P, HEADS])
        eid = a.sb("eid", [P, HK])
        tq = [a.ps(f"tq{b}", [P, 4, P]) for b in range(4)]
        sp_ = [a.ps(f"sp{b}", [P, 4, P]) for b in range(2)]
        tg = a.ps("tg", [P, 3, P])
        q_in, const_in, turned, q_copied, scored, s_copied, found, exps_in, exps = (
            a.sem(x) for x in ("q_in", "const_in", "turned", "q_copied", "scored", "s_copied", "found", "exps_in", "exps"))
        chosen, back, kept, dstep, carried = (a.sem(x) for x in ("chosen", "back", "kept", "dstep", "carried"))
        block = ctx.enter_context(nc.Block())

        @block.sync
        def _(sp):
            sp.dma_start(ident[:], c["ident"]).then_inc(const_in, 16)
            sp.dma_start(kt[:], keys).then_inc(const_in, 16)
            sp.dma_start(iota[:], c["iota"][:, 0:TOPK]).then_inc(const_in, 16)

            def tile(t):
                wait(sp, turned, 4 * t)
                sp.dma_start(q[:], queries[bass.ds(t * P, P), :]).then_inc(q_in, 16)

            tile(0)
            with sp.Fori(1, TILES) as t:
                tile(t)

        @block.tensor
        def _(pe):
            pe.wait_ge(const_in, 48)

            def tile(t):
                pe.wait_ge(q_in, 16 * (t + 1))
                for b in range(4):
                    wait(pe, q_copied, 4 * (t - 1) + b + 1)
                    for n in range(4):
                        ins = nc.tensor.transpose(tq[b][:, n, :], q[:, (4 * b + n) * DQ:(4 * b + n + 1) * DQ], ident[:])
                    ins.then_inc(turned, 1)
                for b in range(4):
                    pe.wait_ge(q_copied, 4 * t + b + 1)
                    wait(pe, s_copied, 4 * t + b - 1)
                    for n in range(4):
                        ins = nc.tensor.matmul(sp_[b % 2][:, n, :], qT[:, 4 * b + n, :], kt[:, 4 * b + n, :], start=True,
                                               stop=True)
                    ins.then_inc(scored, 1)

            def turn_back(t):
                pe.wait_ge(chosen, t + 1)
                wait(pe, kept, 3 * t)
                for n, x in enumerate((picked[0][:], picked[1][:], gate[:].rearrange("p h k -> p (h k)"))):
                    ins = nc.tensor.transpose(tg[:, n, :], x, ident[:])
                ins.then_inc(back, 1)

            tile(0)
            with pe.Fori(1, TILES) as t:
                tile(t)
                turn_back(t - 1)
            turn_back(TILES - 1)

        @block.scalar
        def _(act):
            def tile(t):
                for b in range(4):
                    act.wait_ge(turned, 4 * t + b + 1)
                    wait(act, scored, 4 * t)
                    nc.scalar.copy(qT[:, 4 * b:4 * b + 4, :], tq[b][:]).then_inc(q_copied, 1)
                for b in range(4):
                    act.wait_ge(scored, 4 * t + b + 1)
                    wait(act, found, t)
                    nc.scalar.copy(s[0][:, 4 * b:4 * b + 4, :], sp_[b % 2][:]).then_inc(s_copied, 1)

            def choose(t):
                act.wait_ge(exps_in, t + 1)
                nc.scalar.activation(gate[:], gate[:], ACT.Exp).then_inc(exps, 1)
                act.wait_ge(back, t + 1)
                for n, x in enumerate((firsts, seconds, gates)):
                    nc.scalar.copy(x[:, bass.ds(t * P, P)], tg[:, n, :]).then_inc(kept, 1)

            tile(0)
            with act.Fori(1, TILES) as t:
                tile(t)
                choose(t - 1)
            choose(TILES - 1)
            act.wait_ge(kept, 3 * TILES)

        @block.vector
        def _(vec):
            d = Steps(vec, dstep)
            v, mult = nc.vector, ALU.mult
            vec.wait_ge(const_in, 48)

            def ready():
                vec.sem_inc(carried, 1)

            def top16(rows, vals_of, idx_of, work, spare):
                for n in range(rows):
                    d(v.max(vals_of(n)[:, 0:8], work(n)))
                d.wait()
                ready()
                for n in range(rows):
                    d(v.max_index(idx_of(n)[:, 0:8], vals_of(n)[:, 0:8], work(n)))
                    d(v.match_replace(spare(n), vals_of(n)[:, 0:8], work(n), -3.0e38))
                d.wait()
                ready()
                for n in range(rows):
                    d(v.max(vals_of(n)[:, 8:16], spare(n)))
                d.wait()
                ready()
                for n in range(rows):
                    ins = v.max_index(idx_of(n)[:, 8:16], vals_of(n)[:, 8:16], spare(n))
                    if n < rows - 1:
                        d(ins)
                return ins

            def tile(t):
                d.at(per_tile[0] * t)
                vec.wait_ge(s_copied, 4 * t + 4)
                ready()
                top16(HS, lambda n: vals[:, n, :], lambda n: idx[:, n, :], lambda n: s[0][:, n, :],
                      lambda n: s[1][:, n, :]).then_inc(found, 1)
                vec.wait_ge(found, t + 1)
                d(v.tensor_scalar(idxf[:], idx[:], 1.0, None, mult))
                pair = vals[:].rearrange("p (h s) k -> p h s k", s=2)
                for h in range(HEADS):
                    d(v.tensor_tensor(cand[0][:, h, :].rearrange("p (a b) -> p a b", b=TOPK), bcast(pair[:, h, 0, :], 2, TOPK),
                                      bcast(pair[:, h, 1, :], 1, TOPK), ALU.add))
                d.wait()
                ready()
                d(top16(HEADS, lambda n: top[:, n, :], lambda n: sel[:, n, :], lambda n: cand[0][:, n, :],
                        lambda n: cand[1][:, n, :]))
                d.wait()
                wait(vec, back, t)
                v.tensor_tensor(gate[:], top[:], bcast(top[:, :, 0], 2, TOPK), ALU.subtract).then_inc(exps_in, 1)
                d(v.tensor_scalar(half[0][:], sel[:], 4, None, ALU.logical_shift_right))
                d(v.tensor_scalar(half[1][:], sel[:], TOPK - 1, None, ALU.bitwise_and))
                d.wait()
                for n in range(2):
                    d(v.tensor_scalar(halff[n][:], half[n][:], 1.0, None, mult))
                d.wait()
                for n in range(2):
                    d(v.tensor_tensor(hot[n][:], bcast(halff[n][:].rearrange("p h k -> p (h k)"), 2, TOPK),
                                      bcast(iota[:], 1, HK), ALU.is_equal))
                d.wait()
                ids = idxf[:].rearrange("p (h s) k -> p h s k", s=2)
                for n in range(2):
                    hn = hot[n][:].rearrange("p (h k) j -> p h k j", h=HEADS)
                    d(v.tensor_tensor(hn, hn, bcast(ids[:, :, n, :], 2, TOPK), mult))
                d.wait()
                for n in range(2):
                    d(v.tensor_reduce(picked[n][:], hot[n][:], AX.X, ALU.add))
                vec.wait_ge(exps, t + 1)
                d(v.tensor_reduce(total[:], gate[:], AX.X, ALU.add))
                d.wait()
                d(v.reciprocal(total[:], total[:]))
                d.wait()
                v.tensor_tensor(gate[:], gate[:], bcast(total[:], 2, TOPK), mult).then_inc(chosen, 1)

            per_tile = [0]
            tile(0)
            per_tile[0] = d.n
            vec.wait_ge(chosen, 1)
            d(v.scalar_tensor_tensor(eid[:], picked[0][:], float(NKEYS), picked[1][:], mult, ALU.add))
            d.wait()
            d(v.tensor_scalar(expert_ids[:], eid[:], 1.0, None, mult))
            d(v.tensor_scalar(gates0[:], gate[:].rearrange("p h k -> p (h k)"), 1.0, None, mult))
            d.wait()
            d.offset = d.n - per_tile[0]
            with vec.Fori(1, TILES) as t:
                tile(t)


def gate_matrix(nc, name, c, firsts, seconds, gates, G):
    B = 4
    with ExitStack() as ctx:
        a = Alloc(nc, ctx, name)
        iota = a.sb("iota", [P, P])
        ghi = a.sb("ghi", [P, TP], F32R)
        glo = a.sb("glo", [P, TP])
        col = [a.sb(f"col{n}", [P, B]) for n in range(4)]
        hot2 = [a.sb(f"hot2_{n}", [P, P], F32R) for n in range(B)]
        hot1 = [[a.sb(f"hot1_{n}_{x}", [P, P], F32R) for x in range(2)] for n in range(B)]
        stage = [a.sb(f"stage{n}", [P, NKEYS, 64]) for n in range(2)]
        acc = [a.ps(f"acc{n}", [P, B, P]) for n in range(2)]
        const_in, split, cols, seconds_hot, firsts_hot, made, staged = (
            a.sem(x) for x in ("const_in", "split", "cols", "seconds_hot", "firsts_hot", "made", "staged"))
        stored = [a.sem(f"stored{n}") for n in range(2)]
        seconds_col, carried = a.sem("seconds_col"), a.sem("carried")
        scol = a.sb("scol", [P, B])
        block = ctx.enter_context(nc.Block())
        TURNS = 64 // B

        @block.sync
        def _(sp):
            sp.dma_start(iota[:], c["iota"]).then_inc(const_in, 16)
            for g in range(NG):
                sp.wait_ge(staged, TURNS * (g + 1))
                sp.dma_start(G[g].rearrange("p a t -> p (a t)"),
                             stage[g % 2][:].rearrange("p a t -> p (a t)")).then_inc(stored[g % 2], 16)
            sp.wait_ge(stored[0], 16 * ((NG + 1) // 2))
            sp.wait_ge(stored[1], 16 * (NG // 2))

        @block.gpsimd
        def _(pool):
            pool.wait_ge(const_in, 16)

            def turn(n):
                nc.gpsimd.tensor_copy(scol[:], seconds[:, bass.ds(DENSE0 + n * B, B)]).then_inc(seconds_col, 1)
                pool.wait_ge(seconds_col, n + 1)
                wait(pool, made, n)
                pool.sem_inc(carried, 1)
                for x in range(B):
                    nc.gpsimd.tensor_scalar(hot2[x][:], iota[:], scol[:, x:x + 1], None, ALU.is_equal).then_inc(seconds_hot, 1)
                pool.wait_ge(seconds_hot, B * (n + 1))

            turn(0)
            with pool.Fori(1, ND // B) as n:
                turn(n)

        @block.vector
        def _(vec):
            vec.wait_ge(const_in, 16)
            nc.vector.tensor_copy(ghi[:], gates[:]).then_inc(split, 1)
            vec.wait_ge(split, 1)
            nc.vector.tensor_tensor(glo[:], gates[:], ghi[:].bitcast(F32), ALU.subtract).then_inc(split, 1)
            vec.wait_ge(split, 2)

            def turn(n):
                at = bass.ds(DENSE0 + n * B, B)
                for x, src in enumerate((firsts[:, at], ghi[:, at].bitcast(F32), glo[:, at])):
                    nc.vector.tensor_copy(col[x][:], src).then_inc(cols, 1)
                vec.wait_ge(cols, 3 * (n + 1))
                wait(vec, made, n)
                for x in range(B):
                    for part in range(2):
                        nc.vector.tensor_scalar(hot1[x][part][:], iota[:], col[0][:, x:x + 1], col[1 + part][:, x:x + 1],
                                                ALU.is_equal, ALU.mult).then_inc(firsts_hot, 1)
                vec.wait_ge(firsts_hot, 2 * B * (n + 1))

            turn(0)
            with vec.Fori(1, ND // B) as n:
                turn(n)

        @block.tensor
        def _(pe):
            def turn(n, bank):
                wait(pe, staged, n - 1)
                for x in range(B):
                    pe.wait_ge(seconds_hot, B * n + x + 1)
                    pe.wait_ge(firsts_hot, 2 * B * n + 2 * x + 2)
                    nc.tensor.matmul(acc[bank][:, x, :], hot2[x][:], hot1[x][0][:], start=True, stop=False)
                    last = nc.tensor.matmul(acc[bank][:, x, :], hot2[x][:], hot1[x][1][:], start=False, stop=True)
                last.then_inc(made, 1)

            turn(0, 0)
            turn(1, 1)
            with pe.Fori(1, ND // B // 2) as m:
                turn(2 * m, 0)
                turn(2 * m + 1, 1)

        @block.scalar
        def _(act):
            def turn(g, n, k, bank, s):
                act.wait_ge(made, n + 1)
                dst = stage[s][:, :, bass.ds(B * k, B)].rearrange("p a t -> p t a")
                nc.scalar.copy(dst, acc[bank][:]).then_inc(staged, 1)

            for g in range(NG):
                wait(act, stored[g % 2], 16 * (g // 2))
                with act.Fori(0, TURNS // 2) as k:
                    for bank in range(2):
                        turn(g, TURNS * g + 2 * k + bank, 2 * k + bank, bank, g % 2)


def experts(nc, name, h_hi, h_lo, h_rows, expert_ids, gates0, u_rows, v_rows, u_units, v_units, G, acc, accg):
    UN, GS, mult = 2 * CH, 2 * CH, ALU.mult
    with ExitStack() as ctx:
        a = Alloc(nc, ctx, name)
        raw = [a.sb(f"raw{s}", [P, KT, P]) for s in range(2)]
        whi = [a.sb(f"whi{s}", [P, KT, P], F32R) for s in range(2)]
        wlo = [a.sb(f"wlo{s}", [P, KT, P], F32R) for s in range(2)]
        H_hi = a.sb("h_hi", [P, KT, ND], F32R)
        H_lo = a.sb("h_lo", [P, KT, ND], F32R)
        W_hi = a.sb("w_hi", [P, 2, CH, ND], F32R)
        W_lo = a.sb("w_lo", [P, 2, CH, ND], F32R)
        Gc = [a.sb(f"gc{s}", [P, NG, CH, 64]) for s in range(2)]
        hid = a.sb("hid", [P, ND])
        wt = a.sb("wt", [P, ND])
        row = [a.sb(f"row{s}", [P, D]) for s in range(2)]
        ids8 = [a.sb(f"ids8_{j}", [P, 1], U32) for j in range(GS)]
        dot8 = a.sb("dot8", [P, GS])
        w8 = a.sb("w8", [P, GS])
        dots = a.sb("dots", [P, HK])
        hp = [a.ps(f"hp{b}", [P, 512]) for b in range(2)]
        vp = [a.ps(f"vp{b}", [P, 512]) for b in range(4)]
        (const_in, hi_done, lo_done, hidden, gelus, gated, w_hi_done, w_lo_done, out_bank, added, ids_set, row_used,
         dots_kept, dots_gelu, w_set, weighted0, cleared, carried) = (a.sem(x) for x in (
             "const_in", "hi_done", "lo_done", "hidden", "gelus", "gated", "w_hi_done", "w_lo_done", "out_bank", "added",
             "ids_set", "row_used", "dots_kept", "dots_gelu", "w_set", "weighted0", "cleared", "carried"))
        raw_in = [a.sem(f"raw_in{s}") for s in range(2)]
        g_in = [a.sem(f"g_in{s}") for s in range(2)]
        row_in = [a.gpsimd_dma_sem(f"row_in{s}") for s in range(2)]
        block = ctx.enter_context(nc.Block())

        def number(c_, j):
            return j if isinstance(c_, int) and c_ == 0 else CH + UN * (c_ - 1) + j

        def chunks(eng, body, first, last):
            with eng.Fori(first // 2, last // 2) as m:
                body(2 * m, 0)
                body(2 * m + 1, 1)

        def wait_unit(eng, c_, j):
            if isinstance(c_, int) and c_ == NCH:
                eng.wait_ge(out_bank, 4 * (CH * (c_ - 1) + j + 1))
            elif j < CH:
                eng.wait_ge(hidden, CH * c_ + j + 1)
            else:
                eng.wait_ge(out_bank, 4 * (CH * (c_ - 1) + j - CH + 1))

        def wait_slot(eng, c_, j):
            if j >= 2:
                wait_unit(eng, c_, j - 2)
            elif isinstance(c_, int) and c_ == 1:
                wait_unit(eng, 0, CH - 2 + j)
            elif not isinstance(c_, int) or c_ > 1:
                wait_unit(eng, c_ - 1, UN - 2 + j)

        def filled(n, s):
            return 8 * (n - s) + 16

        @block.sync
        def _(sp):
            sp.dma_start(H_hi[:].bitcast(F32), h_hi).then_inc(const_in, 16)
            sp.dma_start(H_lo[:].bitcast(F32), h_lo).then_inc(const_in, 16)
            sp.dma_start(accg[:], h_rows).then_inc(const_in, 16)

            def gates_of(c_, s):
                wait(sp, gated, CH * (c_ - 1))
                sp.dma_start(Gc[s][:].rearrange("p g a t -> p g (a t)"),
                             G[:, :, bass.ds(CH * c_, CH), :].rearrange("g p a t -> p g (a t)")).then_inc(g_in[s], 16)

            def load(c_, j, units, at):
                wait(sp, lo_done, number(c_, j) - 1)
                sp.dma_start(raw[j % 2][:].rearrange("p a b -> p (a b)"),
                             units[bass.ds(at, 1)].rearrange("a p x -> (a p) x")).then_inc(raw_in[j % 2], 16)

            def body(c_, s):
                gates_of(c_, s)
                for j in range(CH):
                    load(c_, j, u_units, CH * c_ + j)
                if not (isinstance(c_, int) and c_ == 0):
                    for j in range(CH):
                        load(c_, CH + j, v_units, CH * (c_ - 1) + j)

            body(0, 0)
            body(1, 1)
            chunks(sp, body, 2, NCH)
            for j in range(CH):
                load(NCH, j, v_units, CH * (NCH - 1) + j)

        @block.gpsimd
        def _(pool):
            def gathers(c_, table, first):
                if not (isinstance(c_, int) and c_ == 0):
                    for s in range(2):
                        pool.wait_ge(row_in[s], 16 * GS // 2 * c_)
                for j in range(GS):
                    nc.gpsimd.tensor_copy(ids8[j][:], expert_ids[:, bass.ds((c_ - first) * GS + j, 1)]).then_inc(ids_set, 1)
                pool.wait_ge(ids_set, GS * (c_ + 1))
                for j in range(GS):
                    wait(pool, row_used, GS * c_ + j - 1)
                    pool.sem_inc(carried, 1)
                    pool.indirect_dma_start(row[j % 2][:], None, table,
                                            bass.IndirectOffsetOnAxis(ids8[j][:], 0)).then_inc(row_in[j % 2], 16)

            gathers(0, u_rows, 0)
            with pool.Fori(1, NCH // 2) as c_:
                gathers(c_, u_rows, 0)
            with pool.Fori(NCH // 2, NCH) as c_:
                gathers(c_, v_rows, NCH // 2)

        @block.scalar
        def _(act):
            def split_hi(c_, j):
                act.wait_ge(raw_in[j % 2], filled(number(c_, j), j % 2))
                wait_slot(act, c_, j)
                nc.scalar.copy(whi[j % 2][:], raw[j % 2][:]).then_inc(hi_done, 1)

            def split_next(c_, j, units):
                split_hi(*((c_, j + 1) if j + 1 < units else (c_ + 1, 0)))

            def post(c_, par, j):
                k = CH * c_ + j
                act.wait_ge(hidden, k + 1)
                wait(act, gated, k)
                nc.scalar.activation(hid[:], hp[j % 2][:, 0:ND], ACT.Gelu).then_inc(gelus, 1)
                act.wait_ge(gated, k + 1)
                nc.scalar.copy(W_hi[:, par, j, :], wt[:]).then_inc(w_hi_done, 1)

            def body(c_, par):
                units = CH if isinstance(c_, int) and c_ == 0 else UN
                for j in range(units):
                    split_next(c_, j, units)
                    if j < CH:
                        post(c_, par, j)

            split_hi(0, 0)
            body(0, 0)
            body(1, 1)
            chunks(act, body, 2, NCH // 2)
            act.wait_ge(dots_kept, NCH // 2)
            nc.scalar.activation(dots[:], dots[:], ACT.Gelu).then_inc(dots_gelu, 1)
            chunks(act, body, NCH // 2, NCH)
            for j in range(CH - 1):
                split_hi(NCH, j + 1)

        @block.vector
        def _(vec):
            v = nc.vector

            def split_lo(c_, j):
                s = j % 2
                vec.wait_ge(hi_done, number(c_, j) + 1)
                v.tensor_tensor(wlo[s][:], raw[s][:], whi[s][:].bitcast(F32), ALU.subtract).then_inc(lo_done, 1)

            def split_next(c_, j, units):
                split_lo(*((c_, j + 1) if j + 1 < units else (c_ + 1, 0)))

            def u_post(c_, par, j):
                k = CH * c_ + j
                if j == 0:
                    vec.wait_ge(g_in[par], filled(c_, par))
                vec.wait_ge(gelus, k + 1)
                wait(vec, w_lo_done, k)
                v.tensor_tensor(wt[:].rearrange("p (g t) -> p g t", t=64), hid[:].rearrange("p (g t) -> p g t", t=64),
                                Gc[par][:, :, j, :], mult).then_inc(gated, 1)
                vec.wait_ge(w_hi_done, k + 1)
                v.tensor_tensor(W_lo[:, par, j, :], wt[:], W_hi[:, par, j, :].bitcast(F32),
                                ALU.subtract).then_inc(w_lo_done, 1)

            def v_add(c_, j, b):
                k = CH * c_ + j
                vec.wait_ge(out_bank, 4 * k + b + 1)
                wait(vec, added, 4 * (k - CH) + b + 1)
                o = acc[:, 4 * j + b, :]
                v.tensor_tensor(o, o, vp[b][:, 0:ND], ALU.add).then_inc(added, 1)

            def gather_step(c_, j, table):
                s, n = j % 2, GS * c_ + j
                vec.wait_ge(row_in[s], 16 * (GS // 2 * c_ + j // 2 + 1))
                if table == 0:
                    v.tensor_tensor_reduce(row[s][:], row[s][:], accg[:], 1.0, 0.0, mult, ALU.add,
                                           dot8[:, j:j + 1]).then_inc(row_used, 1)
                else:
                    vec.wait_ge(row_used, n)
                    v.scalar_tensor_tensor(accg[:], row[s][:], w8[:, j:j + 1], accg[:], mult, ALU.add).then_inc(row_used, 1)

            def body(c_, par, table=0):
                first = isinstance(c_, int) and c_ == 0
                if table == 1:
                    at = c_ - NCH // 2
                    vec.wait_ge(row_used, GS * c_)
                    v.tensor_scalar(w8[:], dots[:, bass.ds(at * GS, GS)], 1.0, None, mult).then_inc(w_set, 1)
                    vec.wait_ge(w_set, at + 1)
                units = CH if first else UN
                for j in range(units):
                    split_next(c_, j, units)
                    if j < CH:
                        u_post(c_, par, j)
                        for g in ((2 * j, 2 * j + 1) if first else (j,)):
                            gather_step(c_, g, table)
                    else:
                        v_add(c_ - 1, j - CH, 0)
                        v_add(c_ - 1, j - CH, 1)
                        gather_step(c_, j, table)
                        v_add(c_ - 1, j - CH, 2)
                        v_add(c_ - 1, j - CH, 3)
                if table == 0:
                    vec.wait_ge(row_used, GS * (c_ + 1))
                    v.tensor_scalar(dots[:, bass.ds(c_ * GS, GS)], dot8[:], 1.0, None, mult).then_inc(dots_kept, 1)
                    vec.wait_ge(dots_kept, c_ + 1)

            v.memset(acc[:], 0.0).then_inc(cleared, 1)
            vec.wait_ge(cleared, 1)
            vec.wait_ge(const_in, 48)
            split_lo(0, 0)
            body(0, 0)
            body(1, 1)
            chunks(vec, body, 2, NCH // 2)
            v.memset(accg[:], 0.0).then_inc(weighted0, 1)
            vec.wait_ge(dots_gelu, 1)
            v.tensor_tensor(dots[:], dots[:], gates0[:], mult).then_inc(weighted0, 1)
            vec.wait_ge(weighted0, 2)
            chunks(vec, lambda c_, par: body(c_, par, 1), NCH // 2, NCH)
            for j in range(CH):
                if j < CH - 1:
                    split_lo(NCH, j + 1)
                for b in range(4):
                    v_add(NCH - 1, j, b)

        @block.tensor
        def _(pe):
            mm = nc.tensor.matmul
            pe.wait_ge(const_in, 48)

            def u_unit(c_, j):
                s, o, k = j % 2, hp[j % 2][:, 0:ND], CH * c_ + j
                pe.wait_ge(lo_done, number(c_, j) + 1)
                wait(pe, gelus, k - 1)
                for x in range(KT):
                    mm(o, whi[s][:, x, :], H_hi[:, x, :], start=x == 0, stop=False)
                    mm(o, whi[s][:, x, :], H_lo[:, x, :], start=False, stop=False)
                    ins = mm(o, wlo[s][:, x, :], H_hi[:, x, :], start=False, stop=x == KT - 1)
                ins.then_inc(hidden, 1)

            def v_unit(c_, j, place, par):
                s, k = j % 2, CH * (c_ - 1) + j
                pe.wait_ge(lo_done, number(c_, place) + 1)
                if j == 0:
                    pe.wait_ge(w_lo_done, CH * c_)
                for b in range(4):
                    wait(pe, added, 4 * (k - 1) + b + 1)
                    o = vp[b][:, 0:ND]
                    for e in range(CH):
                        hi, lo = whi[s][:, 4 * e + b, :], wlo[s][:, 4 * e + b, :]
                        mm(o, hi, W_hi[:, par, e, :], start=e == 0, stop=False)
                        mm(o, hi, W_lo[:, par, e, :], start=False, stop=False)
                        ins = mm(o, lo, W_hi[:, par, e, :], start=False, stop=e == CH - 1)
                    ins.then_inc(out_bank, 1)

            def body(c_, par):
                for j in range(CH):
                    u_unit(c_, j)
                if not (isinstance(c_, int) and c_ == 0):
                    for j in range(CH):
                        v_unit(c_, j, CH + j, 1 - par)

            body(0, 0)
            body(1, 1)
            chunks(pe, body, 2, NCH)
            for j in range(CH):
                v_unit(NCH, j, j, (NCH - 1) % 2)


def finish(nc, name, c, sums, w_row, acc, accg, y):
    with ExitStack() as ctx:
        a = Alloc(nc, ctx, name)
        X = [a.sb(f"x{t}", [P, D]) for t in range(TILES)]
        W = a.sb("w", [P, D])
        junk = a.sb("junk", [P, D])
        ident = a.sb("ident", [P, P])
        mean, root, rstd, tmp, ss = (a.sb(n, [P, TILES]) for n in ("mean", "root", "rstd", "tmp", "ss"))
        bank = [a.ps(f"t{b}", [P, 4, P]) for b in range(4)]
        loaded = [a.sem(f"loaded{t}") for t in range(TILES)]
        const_in, turned, summed, squared, meaned, rooted, scaled, done, stored, dstep, half_added = (
            a.sem(s) for s in ("const_in", "turned", "summed", "squared", "meaned", "rooted", "scaled", "done", "stored",
                               "dstep", "half_added"))
        block = ctx.enter_context(nc.Block())

        def rows(t):
            return P if t < PTILES else NSMP

        @block.sync
        def _(sp):
            sp.dma_start(ident[:], c["ident"]).then_inc(const_in, 16)
            sp.dma_start(W[:], w_row.partition_broadcast(P)).then_inc(const_in, 16)
            for t in range(TILES):
                sp.dma_start(X[t][:], sums[t * P:(t + 1) * P, :]).then_inc(loaded[t], 16)
            for t in range(TILES):
                sp.wait_ge(done, t + 1)
                sp.dma_start(y[t * P:t * P + rows(t), :], X[t][0:rows(t), :]).then_inc(stored, 16)
            sp.wait_ge(stored, 16 * TILES)

        @block.tensor
        def _(pe):
            pe.wait_ge(const_in, 32)
            for t in range(1, TILES):
                R = rows(t)
                for b in range(4):
                    wait(pe, half_added, 4 * (t - 2) + b + 1)
                    for k in range(4):
                        ins = nc.tensor.transpose(bank[b][0:R, k, :], acc[:, 4 * b + k, (t - 1) * P:(t - 1) * P + R], ident[:])
                    ins.then_inc(turned, 1)

        @block.scalar
        def _(act):
            for t in range(TILES):
                R = rows(t)
                if t == 0:
                    act.wait_ge(summed, 1)
                else:
                    act.wait_ge(half_added, 4 * t)
                wait(act, squared, t)
                nc.scalar.activation(junk[0:R, :], X[t][0:R, :], ACT.Square, accum_out=ss[0:R, t:t + 1]).then_inc(squared, 1)
                act.wait_ge(meaned, t + 1)
                nc.scalar.activation(root[0:R, t:t + 1], mean[0:R, t:t + 1], ACT.Sqrt).then_inc(rooted, 1)

        @block.vector
        def _(vec):
            v, d = nc.vector, Steps(vec, dstep)
            vec.wait_ge(const_in, 32)

            def add(t):
                R = rows(t)
                vec.wait_ge(loaded[t], 16)
                if t == 0:
                    v.tensor_tensor(X[0][:], X[0][:], accg[:], ALU.add).then_inc(summed, 1)
                    return
                for b in range(4):
                    vec.wait_ge(turned, 4 * (t - 1) + b + 1)
                    x = X[t][0:R, 512 * b:512 * (b + 1)].rearrange("p (k f) -> p k f", k=4)
                    v.tensor_tensor(x, x, bank[b][0:R], ALU.add).then_inc(half_added, 1)

            def norm(t):
                R, at = rows(t), slice(t, t + 1)
                vec.wait_ge(squared, t + 1)
                v.tensor_scalar(mean[0:R, at], ss[0:R, at], 1.0 / D, EPS, ALU.mult, ALU.add).then_inc(meaned, 1)
                vec.wait_ge(meaned, t + 1)
                vec.wait_ge(rooted, t + 1)
                newton_rsqrt(nc, d, rstd[0:R, at], mean[0:R, at], root[0:R, at], tmp[0:R, at])
                v.scalar_tensor_tensor(X[t][0:R, :], X[t][0:R, :], rstd[0:R, at], W[0:R, :], ALU.mult,
                                       ALU.mult).then_inc(done, 1)

            add(0)
            for t in range(1, TILES):
                add(t)
                norm(t - 1)
            norm(TILES - 1)


def build(nc, x, w, consts, keys, tables, states, outs):
    def scratch(name, shape):
        return nc.dram_tensor(name, shape, F32, kind="Internal").ap()

    proj, alr = scratch("proj", (TP, PROJ)), scratch("alr", (RANK, TP))
    mix, mixed, sums = scratch("mix", (TP, D)), scratch("mixed", (TP, D)), scratch("sums", (TP, D))
    queries, h_rows = scratch("queries", (TP, D)), scratch("h_rows", (P, D))
    h_hi, h_lo = scratch("h_hi", (P, KT, TP)), scratch("h_lo", (P, KT, TP))
    G = scratch("gate_matrix", (NG, P, NKEYS, 64))
    ident = consts["ident"]

    def parts(ctx, n):
        return [ctx.enter_context(nc.sbuf_tensor(f"rows{n}_{p}", [P, KT, TP], F32R)) for p in ("hi", "lo")]

    with ExitStack() as ctx:
        hi, lo = parts(ctx, 1)
        norm_transpose(nc, "norm1", hi, lo, ident, x, norm=w["norm_mix"])
        stream_matmul(nc, "in_proj", hi, lo, w["in"], proj, small=(w["alr"], alr))
    mixer(nc, "mixer", consts, proj, alr, w["a2"], w["gn"], states, outs["states"], mix)
    with ExitStack() as ctx:
        hi, lo = parts(ctx, 2)
        norm_transpose(nc, "turn_mix", hi, lo, ident, mix)
        stream_matmul(nc, "out_proj", hi, lo, w["out"], mixed)
    with ExitStack() as ctx:
        hi, lo = parts(ctx, 3)
        norm_transpose(nc, "norm2", hi, lo, ident, x, norm=w["norm_ffn"], add=mixed, sum_dst=sums,
                       row=(w["norm_ffn_row"], h_rows), spill=(h_hi, h_lo))
        stream_matmul(nc, "queries", hi, lo, w["pq"], queries)
    with ExitStack() as ctx:
        expert_ids = ctx.enter_context(nc.sbuf_tensor("expert_ids", [P, HK], U32))
        gates0 = ctx.enter_context(nc.sbuf_tensor("gates0", [P, HK], F32))
        with ExitStack() as inner:
            firsts, seconds, gates = (inner.enter_context(nc.sbuf_tensor(n, [P, TP], F32))
                                      for n in ("firsts", "seconds", "gates"))
            route(nc, "route", consts, queries, keys, expert_ids, gates0, firsts, seconds, gates)
            gate_matrix(nc, "gate_matrix", consts, firsts, seconds, gates, G)
        acc = ctx.enter_context(nc.sbuf_tensor("acc", [P, KT, ND], F32))
        accg = ctx.enter_context(nc.sbuf_tensor("accg", [P, D], F32))
        dense = slice(DENSE0, DENSE0 + ND)
        experts(nc, "experts", h_hi[:, :, dense], h_lo[:, :, dense], h_rows, expert_ids, gates0, tables["u_rows"],
                tables["v_rows"], tables["u_units"], tables["v_units"], G, acc, accg)
        finish(nc, "finish", consts, sums, w["norm_final"], acc, accg, outs["y"])


def kernel(**inputs):
    import concourse.bacc as bacc
    from concourse.bass_utils import run_bass_kernel_spmd

    nc = bacc.Bacc("TRN2", target_bir_lowering=False, num_devices=1)
    g = {k: np.asarray(v) for k, v in inputs.items()}
    arrays = {}

    def put(name, array):
        arrays[name] = np.ascontiguousarray(array)
        return nc.dram_tensor(name, arrays[name].shape, mybir.dt.from_np(arrays[name].dtype), kind="ExternalInput").ap()

    def out(name, shape):
        return nc.dram_tensor(name, shape, F32, kind="ExternalOutput").ap()

    def blocks(m):
        return m.reshape(KQ, KT // KQ, P, -1, NB).transpose(3, 0, 2, 1, 4)

    x = np.zeros((TP, D), np.float32)
    x[:SEQ] = g["x_prompt"][0]
    x[SEQ:SEQ + NSMP] = g["x_sample"].reshape(NSMP, D)
    alr = np.zeros((D, P), np.float32)
    alr[:, :RANK] = g["w_in"][0][:, PROJ:]
    w = {
        "norm_mix": put("norm_mix", g["w_norm_mix"][0].reshape(KT, P).T),
        "norm_ffn": put("norm_ffn", g["w_norm_ffn"][0].reshape(KT, P).T),
        "norm_ffn_row": put("norm_ffn_row", g["w_norm_ffn"][0]),
        "norm_final": put("norm_final", g["w_norm_final"]),
        "in": put("w_in", blocks(g["w_in"][0][:, :PROJ])),
        "alr": put("w_alr", alr.reshape(KT, P, P).transpose(1, 0, 2)),
        "out": put("w_out", blocks(g["w_out"][0])),
        "pq": put("w_pq", blocks(g["w_pq"][0])),
        "a2": put("w_a2", np.concatenate([g["w_gla_a2"][0], g["b_gla_a"][0][None]], 0)),
        "gn": put("gn", np.stack([g["gn_ret_w"][0].ravel(), g["gn_ret_b"][0].ravel(), g["gn_gla_w"][0].ravel()])),
    }
    keys = np.stack([g["sub_keys1"][0], g["sub_keys2"][0]], 1)
    keys = put("keys", keys.reshape(2 * HEADS, NKEYS, DQ).transpose(2, 0, 1))
    u, v = g["u_tab"][0], g["v_tab"][0]
    tables = {
        "u_rows": put("u_rows", u),
        "v_rows": put("v_rows", v),
        "u_units": put("u_units", u.reshape(NKEYS, NKEYS, KT, P).transpose(0, 3, 2, 1).reshape(NKEYS, P, D)),
        "v_units": put("v_units", v.reshape(NCH, CH, NKEYS, DS, 512).transpose(0, 3, 2, 1, 4).reshape(NCH * DS, P, D)),
    }
    consts = {k: put(f"const_{k}", a) for k, a in constants().items()}
    states = (put("state_ret", g["state_ret"][0]), put("state_gla", g["state_gla"][0]))
    outs = {
        "y": out("y", (SEQ + NSMP, D)),
        "states": [[out("ret_p", (H, DK, DV)), out("gla_p", (H, DK, DV))],
                   [out("ret_s", (NSEQ, H, DK, DV)), out("gla_s", (NSEQ, H, DK, DV))]],
    }
    build(nc, put("x", x), w, consts, keys, tables, states, outs)
    r = run_bass_kernel_spmd(nc, [arrays], core_ids=[0]).results[0]
    y = r["y"]
    return (y[:SEQ].reshape(1, SEQ, D), y[SEQ:].reshape(NSEQ, LSEQ, D), r["ret_p"].reshape(1, 1, H, DK, DV),
            r["gla_p"].reshape(1, 1, H, DK, DV), r["ret_s"].reshape(1, NSEQ, H, DK, DV),
            r["gla_s"].reshape(1, NSEQ, H, DK, DV))
```

```python
from contextlib import ExitStack

import numpy as np

import concourse.bass as bass
from concourse import mybir

F32 = mybir.dt.float32
F32R = mybir.dt.float32r
U32 = mybir.dt.uint32
ALU = mybir.AluOpType
ACT = mybir.ActivationFunctionType
AX = mybir.AxisListType

P = 128
D = 2048
KT = D // P
SEQ, NSEQ, LSEQ = 512, 8, 8
NSMP = NSEQ * LSEQ
TILES = SEQ // P + 1
PTILES = TILES - 1
TP = TILES * P
PAST = 4096
EPS = 1e-6
H, DK, DV = 4, 128, 256
RANK, TEMP = 16, 16.0
PROJ = 2 * (2 * H * DK + 2 * H * DV)
NB = 512
KQ = 4
QR, KR, VR, GR, QG, KG, VG, GG = 0, 512, 1024, 2048, 3072, 3584, 4096, 5120
SUB, BLK = 8, 32
LOG_A_MIN = -20.0
EXP_MAX = 80.0
HEADS, NKEYS, TOPK, DQ = 8, 128, 16, 128
HK = HEADS * TOPK
DENSE0 = P
ND = PTILES * P - P + NSMP
GT = 32
NG = ND // GT
CH = 4
NCH = NKEYS // CH
DS = D // 512
UB = 8
ROUTE_B = TILES
GATE_B = NG // 2
GATHER_B = NKEYS // UB - ROUTE_B - GATE_B


GAMMA = [1.0 - 2.0 ** (-5 - h) for h in range(H)]


def wait(eng, sem, value):
    if not (isinstance(value, int) and value <= 0):
        eng.wait_ge(sem, value)


class Steps:

    def __init__(self, eng, sem):
        self.eng, self.sem, self.base, self.n, self.offset = eng, sem, 0, 0, 0

    def __call__(self, ins):
        self.n += 1
        ins.then_inc(self.sem, 1)

    def wait(self):
        self.eng.wait_ge(self.sem, self.base + self.n)

    def at(self, base):
        self.base, self.n = base + self.offset, 0


def bcast(ap, axis, count):
    shape = list(ap.shape)
    shape.insert(axis, count)
    return ap.unsqueeze(axis).broadcast_to(shape)


class Alloc:

    def __init__(self, nc, ctx, name):
        self.nc, self.ctx, self.name, self.sems = nc, ctx, name, []
        ctx.callback(self.clear)

    def clear(self):
        for sem in self.sems:
            self.nc.gpsimd.sem_clear(sem)
        self.nc.all_engine_barrier()

    def sb(self, name, shape, dt=F32):
        return self.ctx.enter_context(self.nc.sbuf_tensor(f"{self.name}_{name}", shape, dt))

    def ps(self, name, shape):
        return self.ctx.enter_context(self.nc.psum_tensor(f"{self.name}_{name}", shape, F32))

    def sem(self, name):
        self.sems.append(self.ctx.enter_context(self.nc.semaphore(f"{self.name}_{name}")))
        return self.sems[-1]


    def gpsimd_dma_sem(self, name):
        return self.nc.alloc_semaphore(f"{self.name}_{name}")


def newton_rsqrt(nc, dve, out, mean, root, tmp):
    dve(nc.vector.reciprocal(out, root))
    dve.wait()
    dve(nc.vector.tensor_tensor(tmp, out, out, ALU.mult))
    dve.wait()
    dve(nc.vector.tensor_tensor(tmp, tmp, mean, ALU.mult))
    dve.wait()
    dve(nc.vector.tensor_scalar(tmp, tmp, -0.5, 1.5, ALU.mult, ALU.add))
    dve.wait()
    dve(nc.vector.tensor_tensor(out, out, tmp, ALU.mult))
    dve.wait()


class Weights:

    def __init__(self, nc, ctx, name, dram, small=None):
        self.dram = dram
        self.raw = [ctx.enter_context(nc.sbuf_tensor(f"{name}_raw{s}", [P, KT // KQ, NB], F32)) for s in range(KQ)]
        self.raw_in = [ctx.enter_context(nc.semaphore(f"{name}_raw_in{s}")) for s in range(KQ)]
        self.sems, self.small = list(self.raw_in), None
        if small is not None:
            self.small_dram = small
            self.small = ctx.enter_context(nc.sbuf_tensor(f"{name}_small", [P, KT * P], F32))
            self.small_in = ctx.enter_context(nc.semaphore(f"{name}_small_in"))
            self.sems.append(self.small_in)

    def load_first(self, sp):
        if self.small is not None:
            sp.dma_start(self.small[:], self.small_dram.rearrange("p k n -> p (k n)")).then_inc(self.small_in, 16)
        for q in range(KQ):
            sp.dma_start(self.raw[q][:], self.dram[0, q]).then_inc(self.raw_in[q], 16)


def norm_transpose(nc, name, hi, lo, ident_dram, src, ahead, norm=None, row=None):
    with ExitStack() as ctx:
        a = Alloc(nc, ctx, name)
        X = a.sb("x", [P, TILES, D])
        ident = a.sb("ident", [P, P])
        if norm is not None:
            weight, junk = a.sb("weight", [P, D]), a.sb("junk", [P, D])
            xn = [a.sb(f"xn{s}", [P, D]) for s in range(2)]
            ss, mean, root, rstd, tmp = (a.sb(s, [P, TILES]) for s in ("ss", "mean", "root", "rstd", "tmp"))
        bank = [a.ps(f"t{b}", [P, 4, P]) for b in range(8)]
        x_in = [a.sem(f"x_in{t}") for t in range(TILES)]
        ident_in, weight_in, squared, meaned, rooted, normed = (
            a.sem(s) for s in ("ident_in", "weight_in", "squared", "meaned", "rooted", "normed"))
        turned, hi_done, lo_done, stored, dstep = (a.sem(s) for s in ("turned", "hi_done", "lo_done", "stored", "dstep"))
        block = ctx.enter_context(nc.Block())

        @block.sync
        def _(sp):
            for t in range(TILES):
                sp.dma_start(X[:, t, :], src[t * P:(t + 1) * P, :]).then_inc(x_in[t], 16)
            ahead.load_first(sp)
            if row is not None:
                sp.wait_ge(normed, 1)
                sp.dma_start(row, xn[0][:]).then_inc(stored, 16)
                sp.wait_ge(stored, 16)

        @block.scalar
        def _(act):
            act.dma_start(ident[:], ident_dram).then_inc(ident_in, 16)
            if norm is not None:
                act.dma_start(weight[:], norm.partition_broadcast(P)).then_inc(weight_in, 16)

            def root_of_mean(t):
                act.wait_ge(x_in[t], 16)
                wait(act, squared, t)
                nc.scalar.activation(junk[:], X[:, t, :], ACT.Square, accum_out=ss[:, t:t + 1]).then_inc(squared, 1)
                act.wait_ge(meaned, t + 1)
                nc.scalar.activation(root[:, t:t + 1], mean[:, t:t + 1], ACT.Sqrt).then_inc(rooted, 1)

            def split_hi(t):
                for b in range(4):
                    act.wait_ge(turned, 4 * t + b + 1)
                    nc.scalar.copy(hi[:, 4 * b:4 * b + 4, t * P:(t + 1) * P], bank[4 * (t % 2) + b][:]).then_inc(hi_done, 1)

            for t in range(TILES):
                if norm is not None:
                    root_of_mean(t)
                if t > 0:
                    split_hi(t - 1)
            split_hi(TILES - 1)

        @block.vector
        def _(vec):
            dve = Steps(vec, dstep)

            def scale(t):
                at = slice(t, t + 1)
                vec.wait_ge(squared, t + 1)
                nc.vector.tensor_scalar(mean[:, at], ss[:, at], 1.0 / D, EPS, ALU.mult, ALU.add).then_inc(meaned, 1)
                vec.wait_ge(meaned, t + 1)
                vec.wait_ge(rooted, t + 1)
                newton_rsqrt(nc, dve, rstd[:, at], mean[:, at], root[:, at], tmp[:, at])
                wait(vec, turned, 4 * (t - 1))
                if t == 0:
                    vec.wait_ge(weight_in, 16)
                if t == 2 and row is not None:
                    vec.wait_ge(stored, 16)
                nc.vector.scalar_tensor_tensor(xn[t % 2][:], X[:, t, :], rstd[:, at], weight[:], ALU.mult,
                                               ALU.mult).then_inc(normed, 1)

            def split_lo(t):
                for b in range(4):
                    vec.wait_ge(hi_done, 4 * t + b + 1)
                    part = hi[:, 4 * b:4 * b + 4, t * P:(t + 1) * P]
                    nc.vector.tensor_tensor(lo[:, 4 * b:4 * b + 4, t * P:(t + 1) * P], bank[4 * (t % 2) + b][:],
                                            part.bitcast(F32), ALU.subtract).then_inc(lo_done, 1)

            for t in range(TILES):
                if norm is not None:
                    scale(t)
                if t > 0:
                    split_lo(t - 1)
            split_lo(TILES - 1)

        @block.tensor
        def _(pe):
            pe.wait_ge(ident_in, 16)
            for t in range(TILES):
                if norm is not None:
                    pe.wait_ge(normed, t + 1)
                else:
                    pe.wait_ge(x_in[t], 16)
                rows = xn[t % 2][:] if norm is not None else X[:, t, :]
                for b in range(4):
                    wait(pe, lo_done, 4 * (t - 2) + b + 1)
                    for k in range(4):
                        last = nc.tensor.transpose(bank[4 * (t % 2) + b][:, k, :], rows[:, (4 * b + k) * P:(4 * b + k + 1) * P],
                                                   ident[:])
                    last.then_inc(turned, 1)


def stream_matmul(nc, name, hi, lo, weights, dst, small=None, residual=None, spill=None):
    blocks, ks, halves, ht = weights.dram.shape[0], KT // KQ, 2, TP // 2
    raw, raw_in = weights.raw, weights.raw_in
    with ExitStack() as ctx:
        a = Alloc(nc, ctx, name)
        a.sems.extend(weights.sems)
        whi = [a.sb(f"whi{s}", [P, ks, NB], F32R) for s in range(KQ)]
        wlo = [a.sb(f"wlo{s}", [P, ks, NB], F32R) for s in range(KQ)]
        stage = [a.sb(f"stage{t}", [P, NB]) for t in range(TILES)]
        acc = [a.ps(f"acc{t}", [P, NB]) for t in range(TILES)]
        stored = [a.sem(f"stored{t}") for t in range(TILES)]
        hi_done, lo_done, unit_done, bank_done, staged = (
            a.sem(s) for s in ("hi_done", "lo_done", "unit_done", "bank_done", "staged"))
        if small is not None:
            half = [a.ps(f"half{s}", [P, ht]) for s in range(halves)]
            sstage = a.sb("sstage", [RANK, TP])
            small_hi, small_lo, small_done, small_staged, small_stored = (
                a.sem(f"small_{s}") for s in ("hi", "lo", "done", "staged", "stored"))
            sparts = [x[KQ - 1][:].rearrange("p a b -> p (a b)") for x in (whi, wlo)]
        if residual is not None:
            resid = [a.sb(f"resid{t}", [P, NB]) for t in range(TILES)]
            resid_in = [a.sem(f"resid_in{t}") for t in range(TILES)]
        spilled = a.sem("spilled") if spill is not None else None
        block = ctx.enter_context(nc.Block())

        @block.sync
        def _(sp):
            def load(blk, q):
                sp.wait_ge(lo_done, KQ * (blk - 1) + q + 1)
                sp.dma_start(raw[q][:], weights.dram[blk, q]).then_inc(raw_in[q], 16)

            with sp.Fori(1, blocks) as blk:
                for q in range(KQ):
                    load(blk, q)
            if spill is not None:
                sp.dma_start(spill[0], hi[:].bitcast(F32)).then_inc(spilled, 16)
                sp.dma_start(spill[1], lo[:].bitcast(F32)).then_inc(spilled, 16)
                sp.wait_ge(spilled, 32)

        @block.scalar
        def _(act):
            def split_hi(blk, q):
                act.wait_ge(raw_in[q], 16 * (blk + 1))
                if q < KQ - 1:
                    wait(act, unit_done, (KQ - 1) * (blk - 1) + q + 1)
                else:
                    wait(act, bank_done, TILES * blk)
                nc.scalar.copy(whi[q][:], raw[q][:]).then_inc(hi_done, 1)

            def load_residual(blk, t):
                act.dma_start(resid[t][:], residual[t * P:(t + 1) * P, bass.ds(blk * NB, NB)]).then_inc(resid_in[t], 16)

            def evacuate(blk):
                for t in range(TILES):
                    if residual is None:
                        act.wait_ge(bank_done, TILES * blk + t + 1)
                        wait(act, stored[t], 16 * blk)
                        nc.scalar.copy(stage[t][:], acc[t][:]).then_inc(staged, 1)
                    act.wait_ge(staged, TILES * blk + t + 1)
                    act.dma_start(dst[t * P:(t + 1) * P, bass.ds(blk * NB, NB)], stage[t][:]).then_inc(stored[t], 16)
                    if residual is not None and not (isinstance(blk, int) and blk == blocks - 1):
                        load_residual(blk + 1, t)

            if residual is not None:
                for t in range(TILES):
                    load_residual(0, t)
            if small is not None:
                act.wait_ge(weights.small_in, 16)
                nc.scalar.copy(sparts[0], weights.small[:]).then_inc(small_hi, 1)
            for q in range(KQ - 1):
                split_hi(0, q)
            if small is not None:
                act.wait_ge(small_done, 1)
            split_hi(0, KQ - 1)
            if small is not None:
                for s in range(halves):
                    nc.scalar.copy(sstage[:, s * ht:(s + 1) * ht], half[s][0:RANK, :]).then_inc(small_staged, 1)
                act.wait_ge(small_staged, halves)
                act.dma_start(small, sstage[:]).then_inc(small_stored, 16)
            split_hi(1, 0)
            evacuate(0)
            with act.Fori(1, blocks - 1) as blk:
                for q in range(1, KQ):
                    split_hi(blk, q)
                split_hi(blk + 1, 0)
                evacuate(blk)
            for q in range(1, KQ):
                split_hi(blocks - 1, q)
            evacuate(blocks - 1)
            for t in range(TILES):
                act.wait_ge(stored[t], 16 * blocks)
            if small is not None:
                act.wait_ge(small_stored, 16)

        @block.vector
        def _(vec):
            def split_lo(blk, q):
                vec.wait_ge(hi_done, KQ * blk + q + 1)
                nc.vector.tensor_tensor(wlo[q][:], raw[q][:], whi[q][:].bitcast(F32), ALU.subtract).then_inc(lo_done, 1)

            def add_residual(blk):
                for t in range(TILES):
                    vec.wait_ge(bank_done, TILES * blk + t + 1)
                    vec.wait_ge(resid_in[t], 16 * (blk + 1))
                    wait(vec, stored[t], 16 * blk)
                    nc.vector.tensor_tensor(stage[t][:], acc[t][:], resid[t][:], ALU.add).then_inc(staged, 1)

            if small is not None:
                vec.wait_ge(small_hi, 1)
                nc.vector.tensor_tensor(sparts[1], weights.small[:], sparts[0].bitcast(F32), ALU.subtract).then_inc(small_lo, 1)
            if residual is None:
                with vec.Fori(0, blocks) as blk:
                    for q in range(KQ):
                        split_lo(blk, q)
            else:
                for q in range(KQ):
                    split_lo(0, q)
                split_lo(1, 0)
                add_residual(0)
                with vec.Fori(1, blocks - 1) as blk:
                    for q in range(1, KQ):
                        split_lo(blk, q)
                    split_lo(blk + 1, 0)
                    add_residual(blk)
                for q in range(1, KQ):
                    split_lo(blocks - 1, q)
                add_residual(blocks - 1)

        @block.tensor
        def _(pe):
            if small is not None:
                pe.wait_ge(small_lo, 1)
                for s in range(halves):
                    tok = slice(s * ht, (s + 1) * ht)
                    for k in range(KT):
                        w = [x[:, k * P:(k + 1) * P] for x in sparts]
                        nc.tensor.matmul(half[s][:], w[0], hi[:, k, tok], start=k == 0, stop=False)
                        nc.tensor.matmul(half[s][:], w[0], lo[:, k, tok], start=False, stop=False)
                        last = nc.tensor.matmul(half[s][:], w[1], hi[:, k, tok], start=False, stop=k == KT - 1)
                last.then_inc(small_done, 1)

            def products(blk):
                for q in range(KQ):
                    pe.wait_ge(lo_done, KQ * blk + q + 1)
                    for t in range(TILES):
                        if q == 0:
                            wait(pe, staged, TILES * (blk - 1) + t + 1)
                        tok = slice(t * P, (t + 1) * P)
                        for k in range(ks):
                            kk = q * ks + k
                            first, end = kk == 0, kk == KT - 1
                            nc.tensor.matmul(acc[t][:], hi[:, kk, tok], whi[q][:, k, :], start=first, stop=False)
                            nc.tensor.matmul(acc[t][:], hi[:, kk, tok], wlo[q][:, k, :], start=False, stop=False)
                            last = nc.tensor.matmul(acc[t][:], lo[:, kk, tok], whi[q][:, k, :], start=False, stop=end)
                        if q == KQ - 1:
                            last.then_inc(bank_done, 1)
                    if q < KQ - 1:
                        last.then_inc(unit_done, 1)

            products(0)
            with pe.Fori(1, blocks) as blk:
                products(blk)


def mixer(nc, name, c, proj, alr_dram, w_a2, gn, states, new_states, mix):
    W = 4 * P
    with ExitStack() as ctx:
        a = Alloc(nc, ctx, name)
        qk_r = a.sb("qk_r", [P, 8, DK])
        v_r = a.sb("v_r", [P, H, DV])
        g_r = a.sb("g_r", [P, H * DV])
        qk_g = a.sb("qk_g", [P, 8, DK])
        v_g = a.sb("v_g", [P, H, DV])
        g_g = a.sb("g_g", [P, H * DV])
        parts = [(qk_r, QR), (v_r, VR), (g_r, GR), (qk_g, QG), (v_g, VG), (g_g, GG)]
        ident = a.sb("ident", [P, P])
        rope = a.sb("rope", [P, TILES, 2, DK // 2])
        mask_r = a.sb("mask_r", [P, H, P])
        mask_rs = a.sb("mask_rs", [NSMP, H, NSMP])
        qdec = a.sb("qdec", [P, H, P])
        qdec_s = a.sb("qdec_s", [P, H, NSMP])
        kdec = a.sb("kdec", [P, H])
        kdec_s = a.sb("kdec_s", [NSMP, H])
        causal = a.sb("causal", [P, P])
        causal_s = a.sb("causal_s", [NSMP, NSMP])
        keep = a.sb("keep", [P, W])
        keep_s = a.sb("keep_s", [P, H * NSMP])
        seq_cols = a.sb("seq_cols", [P, NSEQ, NSMP])
        seq_rows = a.sb("seq_rows", [NSMP, NSEQ])
        gnb = a.sb("gnb", [P, 3, H * DV])
        wa2 = a.sb("wa2", [RANK + 1, H * DK])
        alr = a.sb("alr", [RANK + 1, TP])
        consts = [(ident, c["ident"]), (rope, c["rope"]), (mask_r, c["mask_r"]), (mask_rs, c["mask_rs"]),
                  (qdec, c["qdec"]), (qdec_s, c["qdec_s"]), (kdec, c["kdec"]), (kdec_s, c["kdec_s"]),
                  (causal, c["causal"]), (causal_s, c["causal_s"]), (keep, c["keep"]), (keep_s, c["keep_s"]),
                  (seq_cols, c["seq_cols"]), (seq_rows, c["seq_rows"]), (wa2, w_a2)]

        rot = a.sb("rot", [P, 8, DK])
        ra = a.sb("ra", [P, 8, DK // 2])
        rb = a.sb("rb", [P, 8, DK // 2])
        kd = a.sb("kd", [P, H, DK])
        qT = a.sb("qT", [P, H, P])
        kT = a.sb("kT", [P, H, P])
        qdT = a.sb("qdT", [P, H, P])
        at_r = a.sb("at_r", [P, H, P])
        at_g = a.sb("at_g", [P, H, P])
        at_gs = a.sb("at_gs", [NSMP, H, NSMP])
        S_r = a.sb("S_r", [P, H, DV])
        S_g = a.sb("S_g", [P, H, DV])
        stats = a.sb("stats", [P, H, 6])
        mv = a.sb("mv", [P, H, 2])
        var = a.sb("var", [P, H])
        root = a.sb("root", [P, H])
        rstd = a.sb("rstd", [P, H])
        tmp = a.sb("tmp", [P, H])
        silu = a.sb("silu", [P, H * DV])
        out = a.sb("out", [P, 2, H * DV])
        z_abs = a.sb("z_abs", [P, W])
        cum = a.sb("cum", [P, W])
        lna = a.sb("lna", [P, W])
        ND_, NO = 4 * 4 * 4 * BLK, H * (BLK + 2 * BLK + 3 * BLK)
        dec = a.sb("dec", [P, ND_ + NO + W + 3 * H * BLK + W + W])
        klr = a.sb("klr", [P, H, DK])
        sdec = a.sb("sdec", [P, H, NSEQ])
        S8 = [a.sb(f"S8_{s}", [P, NSEQ, DV]) for s in range(2)]
        qm = a.sb("qm", [P, NSEQ, NSMP])
        km = a.sb("km", [NSMP, NSEQ, DK])

        tr = [a.ps(f"tr{b}", [P, 4, P]) for b in range(2)]
        sc = a.ps("sc", [P, 4 * P])
        op = [a.ps(f"o{b}", [P, 2, DV]) for b in range(2)]
        st = [a.ps(f"st{b}", [P, 2, DV]) for b in range(2)]
        zp = a.ps("z", [P, W])

        part_in = [a.sem(f"part_in{n}") for n in range(6)]
        const_in, alr_in, ones_set, zeros_set = (a.sem(s) for s in ("const_in", "alr_in", "ones_set", "zeros_set"))
        (rotated, k_decayed, r_turned, r_copied, q_decayed, r_scored, r_masked, r_out, r_states, r_stepped,
         r_var, r_root, r_silu, r_mixed) = (a.sem(s) for s in (
             "rotated", "k_decayed", "r_turned", "r_copied", "q_decayed", "r_scored", "r_masked", "r_out", "r_states",
             "r_stepped", "r_var", "r_root", "r_silu", "r_mixed"))
        (z_made, z_log, args_made, decays_made, g_turned, g_weighted, g_scored, g_masked, g_out, kl_turned, kl_copied,
         g_states, g_stepped, g_squared, g_var, g_root, g_silu, g_mixed) = (a.sem(s) for s in (
             "z_made", "z_log", "args_made", "decays_made", "g_turned", "g_weighted", "g_scored", "g_masked", "g_out",
             "kl_turned", "kl_copied", "g_states", "g_stepped", "g_squared", "g_var", "g_root", "g_silu", "g_mixed"))
        r_mix_stored, g_mix_stored = a.gpsimd_dma_sem("r_mix_stored"), a.gpsimd_dma_sem("g_mix_stored")
        s8_in = [a.gpsimd_dma_sem(f"s8_in{s}") for s in range(2)]
        s8_out = [a.gpsimd_dma_sem(f"s8_out{s}") for s in range(2)]
        q_masked, k_masked, seq_states, seq_stepped = (a.sem(s) for s in ("q_masked", "k_masked", "seq_states", "seq_stepped"))
        final_out, dstep, astep = a.sem("final_out"), a.sem("dstep"), a.sem("astep")
        block = ctx.enter_context(nc.Block())

        def rows(t):
            return P if not (isinstance(t, int) and t == PTILES) else NSMP

        def seg(t, kind):
            R = rows(t)
            G = R // BLK
            size = {"D": H * G * 4 * BLK, "O1": H * BLK, "O2": 2 * H * BLK, "O3": 3 * H * BLK,
                    "Q8": H * R, "QO": 3 * H * BLK, "QC": H * R, "KL": H * R}
            at = 0
            for k, n in size.items():
                if R == NSMP and k in ("O1", "O2", "O3", "QO"):
                    continue
                if k == kind:
                    return dec[:, at:at + n]
                at += n
            return at

        n_consts = len(consts) + 3

        @block.sync
        def _(sp):
            for tile_, src in consts:
                sp.dma_start(tile_[:], src).then_inc(const_in, 16)
            for n in range(3):
                sp.dma_start(gnb[:, n, :], gn[n].partition_broadcast(P)).then_inc(const_in, 16)
            sp.wait_ge(ones_set, 1)
            sp.dma_start(alr[0:RANK, :], alr_dram).then_inc(alr_in, 16)

            def load(t, n, used, count):
                if not (isinstance(t, int) and t == 0):
                    sp.wait_ge(used, count)
                R = rows(t)
                buf, col = parts[n]
                flat = buf[:].rearrange("p a b -> p (a b)") if len(buf.shape) == 3 else buf[:]
                sp.dma_start(flat[0:R, :], proj[bass.ds(t * P, R), col:col + 1024]).then_inc(part_in[n], 16)

            def tile(t):
                load(t, 0, rotated, 2 * t)
                load(t, 1, r_states, t)
                load(t, 2, r_silu, t)
                load(t, 3, g_turned, t)
                load(t, 4, g_states, t)
                load(t, 5, g_silu, t)

            tile(0)
            with sp.Fori(1, PTILES) as t:
                tile(t)
            tile(PTILES)
            for n in range(2):
                S = (S_r, S_g)[n]
                sp.wait_ge((r_stepped, g_stepped)[n], PTILES)
                sp.dma_start(new_states[0][n].rearrange("h d v -> d h v"), S[:]).then_inc(final_out, 16)
            sp.wait_ge(final_out, 32)

        @block.gpsimd
        def _(pool):
            def move_in(n):
                s, group, h = n % 2, n // H, n % H
                wait(pool, s8_out[s], 16 * (n // 2))
                pool.dma_start(S8[s][:], states[group][:, h].rearrange("b d v -> d b v")).then_inc(s8_in[s], 16)

            def store_mix(t, group):
                pool.wait_ge((r_mixed, g_mixed)[group], t + 1)
                pool.dma_start(mix[bass.ds(t * P, P), group * 1024:(group + 1) * 1024], out[:, group, :]).then_inc(
                    (r_mix_stored, g_mix_stored)[group], 16)

            move_in(0)
            move_in(1)
            with pool.Fori(0, PTILES) as t:
                store_mix(t, 0)
                store_mix(t, 1)
            for n in range(2 * H):
                s, group, h = n % 2, n // H, n % H
                pool.wait_ge(seq_stepped, 4 * (n + 1))
                pool.dma_start(new_states[1][group][:, h].rearrange("b d v -> d b v"), S8[s][:]).then_inc(s8_out[s], 16)
                if n + 2 < 2 * H:
                    move_in(n + 2)
                if n % H == H - 1:
                    store_mix(PTILES, group)
            for s in range(2):
                pool.wait_ge(s8_out[s], 16 * H)
            pool.wait_ge(r_mix_stored, 16 * TILES)
            pool.wait_ge(g_mix_stored, 16 * TILES)

        @block.scalar
        def _(act):
            step = Steps(act, astep)
            act.wait_ge(const_in, 16 * n_consts)

            def tile(t):
                R = rows(t)
                step.at(5 * t)
                cols = slice(0, R)
                act.wait_ge(r_turned, t + 1)
                wait(act, r_scored, t)
                nc.scalar.copy(qT[:, :, cols], tr[0][:, :, cols]).then_inc(r_copied, 1)
                nc.scalar.copy(kT[:, :, cols], tr[1][:, :, cols]).then_inc(r_copied, 1)
                act.wait_ge(z_made, t + 1)
                wait(act, z_log, t)
                zl, zr = z_abs[:, 0:H * R], zp[:, 0:H * R]
                step(nc.scalar.activation(zl, zr, ACT.Abs))
                step.wait()
                step(nc.scalar.activation(zl, zl, ACT.Exp, scale=-1.0))
                step.wait()
                nc.scalar.activation(zl, zl, ACT.Ln, bias=1.0).then_inc(z_log, 1)
                act.wait_ge(args_made, t + 1)
                n = seg(t, None)
                nc.scalar.activation(dec[:, 0:n], dec[:, 0:n], ACT.Exp).then_inc(decays_made, 1)
                act.wait_ge(r_var, t + 1)
                nc.scalar.activation(root[0:R, :], var[0:R, :], ACT.Sqrt).then_inc(r_root, 1)
                act.wait_ge(part_in[2], 16 * (t + 1))
                wait(act, g_mixed, t)
                nc.scalar.activation(silu[0:R, :], g_r[0:R, :], ACT.Silu).then_inc(r_silu, 1)
                act.wait_ge(kl_turned, t + 1)
                nc.scalar.copy(klr[0:R, :, :], tr[0][0:R, :, :]).then_inc(kl_copied, 1)
                act.wait_ge(g_out, t + 1)
                act.wait_ge(decays_made, t + 1)
                for h in range(H):
                    ins = nc.scalar.activation(z_abs[0:R, 0:DV], op[h // 2][0:R, h % 2, :], ACT.Square,
                                               accum_out=mv[0:R, h, 0:1])
                    if h < H - 1:
                        step(ins)
                        step.wait()
                ins.then_inc(g_squared, 1)
                act.wait_ge(g_var, t + 1)
                nc.scalar.activation(root[0:R, :], var[0:R, :], ACT.Sqrt).then_inc(g_root, 1)
                act.wait_ge(part_in[5], 16 * (t + 1))
                act.wait_ge(r_mixed, t + 1)
                nc.scalar.activation(silu[0:R, :], g_g[0:R, :], ACT.Silu).then_inc(g_silu, 1)

            tile(0)
            with act.Fori(1, PTILES) as t:
                tile(t)
            tile(PTILES)

        @block.vector
        def _(vec):
            d = Steps(vec, dstep)
            tt, mult = nc.vector.tensor_tensor, ALU.mult
            nc.vector.memset(alr[:], 1.0).then_inc(ones_set, 1)
            for z in (S_r, S_g, at_g, at_gs):
                nc.vector.memset(z[:], 0.0).then_inc(zeros_set, 1)
            vec.wait_ge(zeros_set, 4)
            vec.wait_ge(const_in, 16 * n_consts)

            def finish_group(t, group, weight):
                R = rows(t)
                o = out[0:R, group, :]
                d(tt(o, o, gnb[0:R, weight, :], mult))
                d.wait()
                if group == 0:
                    d(tt(o, o, gnb[0:R, 1, :], ALU.add))
                    d.wait()
                vec.wait_ge((r_silu, g_silu)[group], t + 1)
                tt(o, o, silu[0:R, :], mult).then_inc((r_mixed, g_mixed)[group], 1)

            def sample_head(n, group, h, qsrc, ksrc):
                s = n % 2
                vec.wait_ge((q_decayed, g_weighted)[group], PTILES + 1)
                vec.wait_ge(k_decayed, PTILES + 1)
                wait(vec, seq_states, 2 * n)
                tt(qm[:], bcast(qsrc, 1, NSEQ), seq_cols[:], mult).then_inc(q_masked, 1)
                tt(km[:], bcast(ksrc, 1, NSEQ), bcast(seq_rows[:], 2, DK), mult).then_inc(k_masked, 1)
                for half in range(2):
                    vec.wait_ge(seq_states, 2 * n + half + 1)
                    if half == 0:
                        vec.wait_ge(s8_in[s], 16 * (n // 2 + 1))
                    for pair in range(2):
                        b = 4 * half + 2 * pair
                        S = S8[s][:, b:b + 2, :]
                        if group == 0:
                            nc.vector.scalar_tensor_tensor(S, S, GAMMA[h] ** LSEQ, st[pair][:], mult,
                                                           ALU.add).then_inc(seq_stepped, 1)
                        else:
                            for x in range(2):
                                ins = nc.vector.scalar_tensor_tensor(S[:, x, :], S[:, x, :], sdec[:, h, b + x:b + x + 1],
                                                                     st[pair][:, x, :], mult, ALU.add)
                                if x == 0:
                                    d(ins)
                            ins.then_inc(seq_stepped, 1)

            def tile(t):
                R = rows(t)
                smp = R == NSMP
                G = R // BLK
                cols = slice(0, R)
                d.at(per_tile[0] * t)
                vec.wait_ge(part_in[0], 16 * (t + 1))
                cos = bcast(rope[0:R, bass.ds(t, 1), 0, :].rearrange("p a f -> p (a f)"), 1, 8)
                sin = bcast(rope[0:R, bass.ds(t, 1), 1, :].rearrange("p a f -> p (a f)"), 1, 8)
                x1, x2 = qk_r[0:R, :, 0:64], qk_r[0:R, :, 64:128]
                wait(vec, r_turned, t)
                wait(vec, k_decayed, t)
                d(tt(ra[0:R], x1, cos, mult))
                d(tt(rb[0:R], x2, sin, mult))
                d.wait()
                tt(rot[0:R, :, 0:64], ra[0:R], rb[0:R], ALU.subtract).then_inc(rotated, 1)
                vec.wait_ge(rotated, 2 * t + 1)
                d(tt(ra[0:R], x1, sin, mult))
                d(tt(rb[0:R], x2, cos, mult))
                d.wait()
                tt(rot[0:R, :, 64:128], ra[0:R], rb[0:R], ALU.add).then_inc(rotated, 1)
                vec.wait_ge(rotated, 2 * t + 2)
                wait(vec, r_states, t)
                tt(kd[0:R], rot[0:R, 4:8, :], bcast((kdec_s if smp else kdec)[:], 2, DK), mult).then_inc(k_decayed, 1)
                vec.wait_ge(r_copied, 2 * t + 1)
                wait(vec, r_out, t)
                tt(qdT[:, :, cols], tr[0][:, :, cols], (qdec_s if smp else qdec)[:], mult).then_inc(q_decayed, 1)
                vec.wait_ge(z_log, t + 1)
                zl, zr, la, cu = z_abs[:, 0:H * R], zp[:, 0:H * R], lna[:, 0:H * R], cum[:, 0:H * R]
                d(nc.vector.scalar_tensor_tensor(la, zr, 0.0, zl, ALU.min, ALU.subtract))
                d.wait()
                d(nc.vector.tensor_scalar(la, la, 1.0 / TEMP, LOG_A_MIN, mult, ALU.max))
                d.wait()
                d(nc.vector.tensor_tensor_scan(cu, (keep_s if smp else keep)[:], la, 0.0, mult, ALU.add))
                d.wait()
                vec.wait_ge(r_scored, t + 1)
                wait(vec, r_out, t)
                scv = sc[0:R, 0:H * R].rearrange("p (h i) -> p h i", h=H)
                tt(at_r[0:R, :, cols], scv, (mask_rs if smp else mask_r)[:], mult).then_inc(r_masked, 1)
                wait(vec, g_out, t)
                wait(vec, kl_turned, t)
                sub = ALU.subtract
                c3 = cu.rearrange("p (h i) -> p h i", h=H)
                ref8 = cu.rearrange("p (s i) -> p s i", i=SUB)[:, :, SUB // 2 - 1]
                D = seg(t, "D").rearrange("p (b s j) -> p b s j", s=4, j=BLK)
                d(tt(D, bcast(ref8.rearrange("p (b s) -> p b s", s=4), 3, BLK),
                     bcast(cu.rearrange("p (b j) -> p b j", j=BLK), 2, 4), sub))
                d(tt(seg(t, "Q8").rearrange("p (s i) -> p s i", i=SUB), cu.rearrange("p (s i) -> p s i", i=SUB),
                     bcast(ref8, 2, SUB), sub))
                if not smp:
                    for g in (1, 2, 3):
                        ref = c3[:, :, BLK * g - 1]
                        O = seg(t, f"O{g}").rearrange("p (h j) -> p h j", h=H)
                        d(tt(O, bcast(ref, 2, BLK * g), c3[:, :, 0:BLK * g], sub))
                    refs = cu.rearrange("p (h g i) -> p h g i", h=H, i=BLK)
                    d(tt(seg(t, "QO").rearrange("p (h g i) -> p h g i", h=H, i=BLK), refs[:, :, 1:4, :],
                         bcast(refs[:, :, 0:3, BLK - 1], 3, BLK), sub))
                    last = bcast(c3[:, :, R - 1], 2, R)
                    d(tt(seg(t, "KL").rearrange("p (h i) -> p h i", h=H), last, c3, sub))
                else:
                    seqs = cu.rearrange("p (s i) -> p s i", i=LSEQ)
                    d(tt(seg(t, "KL").rearrange("p (s i) -> p s i", i=LSEQ), bcast(seqs[:, :, LSEQ - 1], 2, LSEQ), seqs, sub))
                d(nc.vector.tensor_scalar(seg(t, "QC"), cu, 1.0, None, mult))
                d.wait()
                Df = seg(t, "D")
                nc.vector.tensor_scalar(Df, Df, EXP_MAX, None, ALU.min).then_inc(args_made, 1)
                if not smp:
                    vec.wait_ge(r_states, t + 1)
                    for h in range(H):
                        ins = nc.vector.scalar_tensor_tensor(S_r[:, h, :], S_r[:, h, :], GAMMA[h] ** P, st[h // 2][:, h % 2, :],
                                                             mult, ALU.add)
                        if h < H - 1:
                            d(ins)
                    ins.then_inc(r_stepped, 1)
                else:
                    for h in range(H):
                        sample_head(h, 0, h, qdT[:, h, cols], kd[0:R, h, :])
                vec.wait_ge(r_out, t + 1)
                for h in range(H):
                    d(nc.vector.bn_stats(stats[0:R, h, :], op[h // 2][0:R, h % 2, :]))
                d.wait()
                ev, od = stats[0:R, :, 0:3], stats[0:R, :, 3:6]
                d(tt(mv[0:R, :, 0], ev[:, :, 1], od[:, :, 1], ALU.add))
                d(tt(mv[0:R, :, 1], ev[:, :, 1], od[:, :, 1], ALU.subtract))
                d(tt(var[0:R, :], ev[:, :, 2], od[:, :, 2], ALU.add))
                d.wait()
                d(nc.vector.tensor_scalar(mv[0:R, :, 0], mv[0:R, :, 0], 0.5, None, mult))
                d(nc.vector.scalar_tensor_tensor(tmp[0:R, :], mv[0:R, :, 1], 0.25, mv[0:R, :, 1], mult, mult))
                d(nc.vector.tensor_scalar(var[0:R, :], var[0:R, :], 1.0 / DV, EPS, mult, ALU.add))
                d.wait()
                tt(var[0:R, :], var[0:R, :], tmp[0:R, :], ALU.add).then_inc(r_var, 1)
                vec.wait_ge(r_var, t + 1)
                vec.wait_ge(r_root, t + 1)
                newton_rsqrt(nc, d, rstd[0:R], var[0:R], root[0:R], tmp[0:R])
                wait(vec, r_mix_stored, 16 * t)
                for h in range(H):
                    d(nc.vector.tensor_scalar(out[0:R, 0, h * DV:(h + 1) * DV], op[h // 2][0:R, h % 2, :], mv[0:R, h, 0:1],
                                              rstd[0:R, h:h + 1], sub, mult))
                d.wait()
                finish_group(t, 0, 0)
                vec.wait_ge(decays_made, t + 1)
                vec.wait_ge(g_turned, t + 1)
                qs, ks = tr[0][:, :, cols], tr[1][:, :, cols]
                h3 = lambda x: x.rearrange("p (h i) -> p h i", h=H)
                stt, scale = nc.vector.scalar_tensor_tensor, DK ** -0.5
                if smp:
                    d(nc.vector.tensor_copy(sdec[:], seg(t, "QC").rearrange("p (h s i) -> p h s i", h=H, i=LSEQ)[:, :, :, LSEQ - 1]))
                else:
                    d(nc.vector.tensor_copy(sdec[:, :, 0], h3(seg(t, "QC"))[:, :, R - 1]))
                d.wait()
                for b in range(H):
                    Db = D[:, b * G:(b + 1) * G]
                    d(tt(Db, Db, bcast(ks[:, b, :].rearrange("p (g j) -> p g j", j=BLK), 2, 4), mult))
                d(stt(h3(seg(t, "Q8")), h3(seg(t, "Q8")), scale, qs, mult, mult))
                d(stt(h3(seg(t, "QC")), h3(seg(t, "QC")), scale, qs, mult, mult))
                if not smp:
                    for g in (1, 2, 3):
                        O = h3(seg(t, f"O{g}"))
                        d(tt(O, O, ks[:, :, 0:BLK * g], mult))
                    d(stt(h3(seg(t, "QO")), h3(seg(t, "QO")), scale, qs[:, :, BLK:R], mult, mult))
                tt(h3(seg(t, "KL")), h3(seg(t, "KL")), ks, mult).then_inc(g_weighted, 1)
                vec.wait_ge(g_scored, t + 1)
                dst, msk = (at_gs, causal_s) if smp else (at_g, causal)
                for g in range(G):
                    r = slice(BLK * g, BLK * (g + 1))
                    cc = slice(BLK * g, BLK * (g + 1) if smp else R)
                    n = cc.stop - cc.start
                    ins = tt(dst[r, :, cc], scv[r, :, cc], bcast(msk[r, cc], 1, H), mult)
                    if g < G - 1:
                        d(ins)
                ins.then_inc(g_masked, 1)
                if smp:
                    vec.wait_ge(kl_copied, t + 1)
                    for h in range(H):
                        sample_head(H + h, 1, h, h3(seg(t, "QC"))[:, h, :], klr[0:R, h, :])
                vec.wait_ge(g_squared, t + 1)
                nc.vector.tensor_scalar(var[0:R, :], mv[0:R, :, 0], 1.0 / DV, EPS, mult, ALU.add).then_inc(g_var, 1)
                vec.wait_ge(g_var, t + 1)
                vec.wait_ge(g_root, t + 1)
                newton_rsqrt(nc, d, rstd[0:R], var[0:R], root[0:R], tmp[0:R])
                wait(vec, g_mix_stored, 16 * t)
                for h in range(H):
                    d(nc.vector.tensor_scalar(out[0:R, 1, h * DV:(h + 1) * DV], op[h // 2][0:R, h % 2, :],
                                              rstd[0:R, h:h + 1], None, mult))
                d.wait()
                finish_group(t, 1, 2)
                if not smp:
                    vec.wait_ge(g_states, t + 1)
                    for h in range(H):
                        ins = stt(S_g[:, h, :], S_g[:, h, :], sdec[:, h, 0:1], st[h // 2][:, h % 2, :], mult, ALU.add)
                        if h < H - 1:
                            d(ins)
                    ins.then_inc(g_stepped, 1)

            per_tile = [0]
            tile(0)
            per_tile[0] = d.n
            with vec.Fori(1, PTILES) as t:
                tile(t)
            tile(PTILES)

        @block.tensor
        def _(pe):
            mm = nc.tensor.matmul
            pe.wait_ge(const_in, 16 * n_consts)
            pe.wait_ge(alr_in, 16)
            pe.wait_ge(zeros_set, 4)

            def tile(t):
                R = rows(t)
                smp = R == NSMP
                G = R // BLK
                wait(pe, z_log, t)
                wait(pe, args_made, t)
                for h in range(H):
                    ins = mm(zp[:, h * R:(h + 1) * R], wa2[:, h * DK:(h + 1) * DK], alr[:, bass.ds(t * P, R)],
                             start=True, stop=True)
                ins.then_inc(z_made, 1)
                pe.wait_ge(rotated, 2 * t + 2)
                wait(pe, kl_copied, t)
                for n in range(8):
                    ins = nc.tensor.transpose(tr[n // 4][:, n % 4, 0:R], rot[0:R, n, :], ident[0:R, 0:R])
                ins.then_inc(r_turned, 1)
                pe.wait_ge(r_copied, 2 * t + 2)
                wait(pe, g_masked, t)
                for h in range(H):
                    ins = mm(sc[0:R, h * R:(h + 1) * R], kT[:, h, 0:R], qT[:, h, 0:R], start=True, stop=True)
                ins.then_inc(r_scored, 1)
                pe.wait_ge(q_decayed, t + 1)
                pe.wait_ge(part_in[3], 16 * (t + 1))
                for n in range(8):
                    ins = nc.tensor.transpose(tr[n // 4][:, n % 4, 0:R], qk_g[0:R, n, :], ident[0:R, 0:R])
                ins.then_inc(g_turned, 1)
                pe.wait_ge(r_masked, t + 1)
                pe.wait_ge(part_in[1], 16 * (t + 1))
                wait(pe, g_mixed, t)
                wait(pe, r_stepped, t)
                if not smp:
                    for h in range(H):
                        o = op[h // 2][0:R, h % 2, :]
                        mm(o, at_r[0:R, h, 0:R], v_r[0:R, h, :], start=True, stop=False)
                        ins = mm(o, qdT[:, h, 0:R], S_r[:, h, :], start=False, stop=True)
                    ins.then_inc(r_out, 1)
                    pe.wait_ge(k_decayed, t + 1)
                    wait(pe, g_stepped, t)
                    for h in range(H):
                        ins = mm(st[h // 2][:, h % 2, :], kd[0:R, h, :], v_r[0:R, h, :], start=True, stop=True)
                    ins.then_inc(r_states, 1)
                else:
                    pe.wait_ge(g_stepped, PTILES)
                    sample_heads(0, at_r, v_r, r_out)
                pe.wait_ge(g_weighted, t + 1)
                D = seg(t, "D").rearrange("p (h g s j) -> p h g s j", h=H, s=4, j=BLK)
                h3 = lambda x: x.rearrange("p (h i) -> p h i", h=H)
                for h in range(H):
                    for g in range(G):
                        for s in range(BLK // SUB):
                            i = BLK * g + SUB * s
                            ins = mm(sc[BLK * g:BLK * (g + 1), h * R + i:h * R + i + SUB], D[:, h, g, s, :],
                                     h3(seg(t, "Q8"))[:, h, i:i + SUB], start=True, stop=True)
                        if g > 0 and not smp:
                            ins = mm(sc[0:BLK * g, h * R + BLK * g:h * R + BLK * (g + 1)], h3(seg(t, f"O{g}"))[:, h, :],
                                     h3(seg(t, "QO"))[:, h, BLK * (g - 1):BLK * g], start=True, stop=True)
                ins.then_inc(g_scored, 1)
                for h in range(H):
                    ins = nc.tensor.transpose(tr[0][0:R, h, :], h3(seg(t, "KL"))[:, h, :], ident[:])
                ins.then_inc(kl_turned, 1)
                pe.wait_ge(g_masked, t + 1)
                pe.wait_ge(part_in[4], 16 * (t + 1))
                pe.wait_ge(r_mixed, t + 1)
                if not smp:
                    for h in range(H):
                        o = op[h // 2][0:R, h % 2, :]
                        mm(o, at_g[0:R, h, 0:R], v_g[0:R, h, :], start=True, stop=False)
                        ins = mm(o, h3(seg(t, "QC"))[:, h, :], S_g[:, h, :], start=False, stop=True)
                    ins.then_inc(g_out, 1)
                    pe.wait_ge(kl_copied, t + 1)
                    pe.wait_ge(r_stepped, t + 1)
                    for h in range(H):
                        ins = mm(st[h // 2][:, h % 2, :], klr[0:R, h, :], v_g[0:R, h, :], start=True, stop=True)
                    ins.then_inc(g_states, 1)
                else:
                    sample_heads(1, at_gs, v_g, g_out)

            def sample_heads(group, at, v, done):
                R = NSMP
                for h in range(H):
                    n = H * group + h
                    o = op[h // 2][0:R, h % 2, :]
                    mm(o, at[0:R, h, 0:R], v[0:R, h, :], start=True, stop=False)
                    pe.wait_ge(s8_in[n % 2], 16 * (n // 2 + 1))
                    pe.wait_ge(q_masked, n + 1)
                    for b in range(NSEQ):
                        ins = mm(o, qm[:, b, :], S8[n % 2][:, b, :], start=False, stop=b == NSEQ - 1)
                    if h == H - 1:
                        ins.then_inc(done, 1)
                    pe.wait_ge(k_masked, n + 1)
                    for half in range(2):
                        wait(pe, seq_stepped, 4 * n + 2 * half)
                        for b in range(4):
                            ins = mm(st[b // 2][:, b % 2, :], km[:, 4 * half + b, :], v[0:R, h, :], start=True, stop=True)
                        ins.then_inc(seq_states, 1)

            tile(0)
            with pe.Fori(1, PTILES) as t:
                tile(t)
            tile(PTILES)


def constants():
    f = np.float32
    pos = np.concatenate([np.arange(SEQ), np.tile(PAST + np.arange(LSEQ), NSEQ), np.zeros(TP - SEQ - NSMP)]).astype(f)
    freqs = (10000.0 ** (-np.arange(0, DK, 2) / DK)).astype(f)
    ang = (pos[:, None] * freqs[None, :]).astype(f)
    rope = np.stack([np.cos(ang.astype(np.float64)), np.sin(ang.astype(np.float64))], 1)
    rope = rope.reshape(TILES, P, 2, DK // 2).transpose(1, 0, 2, 3)
    lg = np.log1p(-np.exp2(-5.0 - np.arange(H)))
    scale = DK ** -0.5

    def masks(L, n):
        i = np.arange(L * n)
        dist = i[None, :] - i[:, None]
        ok = (dist >= 0) & (i[None, :] // L == i[:, None] // L)
        decay = np.where(ok[None], np.exp(np.maximum(dist, 0)[None] * lg[:, None, None]), 0.0) * scale
        q = np.exp((i % L + 1)[None, :] * lg[:, None])
        k = np.exp((L - 1 - i % L)[None, :] * lg[:, None]) * scale
        return (ok, decay.transpose(1, 0, 2), np.broadcast_to(q[None], (P, H, L * n)), k.T)

    ok, mask_r, qdec, kdec = masks(P, 1)
    ok_s, mask_rs, qdec_s, kdec_s = masks(LSEQ, NSEQ)
    keep = np.ones((P, H, P))
    keep[:, :, 0] = 0
    keep_s = np.ones((P, H * NSEQ, LSEQ))
    keep_s[:, :, 0] = 0
    seq = np.arange(NSMP)[None, :] // LSEQ == np.arange(NSEQ)[:, None]
    out = dict(ident=np.eye(P), rope=rope, mask_r=mask_r, mask_rs=mask_rs, qdec=qdec, qdec_s=qdec_s, kdec=kdec,
               kdec_s=kdec_s, causal=ok, causal_s=ok_s, keep=keep.reshape(P, -1), keep_s=keep_s.reshape(P, -1),
               seq_cols=np.broadcast_to(seq[None], (P, NSEQ, NSMP)), seq_rows=seq.T,
               iota=np.broadcast_to(np.arange(P)[None], (P, P)))
    return {k: np.ascontiguousarray(v, dtype=f) for k, v in out.items()}


class Units:

    def __init__(self, nc, a, per):
        self.nc, self.per = nc, per
        self.raw = [a.sb(f"raw{s}", [P, KT, P]) for s in range(2)]
        self.hi = [a.sb(f"whi{s}", [P, KT, P], F32R) for s in range(2)]
        self.lo = [a.sb(f"wlo{s}", [P, KT, P], F32R) for s in range(2)]
        self.raw_in = [a.sem(f"raw_in{s}") for s in range(2)]
        self.hi_done, self.lo_done, self.done = a.sem("hi_done"), a.sem("lo_done"), a.sem("unit_done")

    def load(self, eng, n, s, table, at):
        wait(eng, self.lo_done, n - 1)
        eng.dma_start(self.raw[s][:].rearrange("p a b -> p (a b)"),
                      table[bass.ds(at, 1)].rearrange("a p x -> (a p) x")).then_inc(self.raw_in[s], 16)

    def split_hi(self, act, n, s):
        act.wait_ge(self.raw_in[s], filled(n, s))
        wait(act, self.done, self.per * (n - 1))
        self.nc.scalar.copy(self.hi[s][:], self.raw[s][:]).then_inc(self.hi_done, 1)

    def split_lo(self, vec, n, s):
        vec.wait_ge(self.hi_done, n + 1)
        self.nc.vector.tensor_tensor(self.lo[s][:], self.raw[s][:], self.hi[s][:].bitcast(F32),
                                     ALU.subtract).then_inc(self.lo_done, 1)

    def ready(self, pe, n):
        pe.wait_ge(self.lo_done, n + 1)


def filled(n, s):
    return 8 * (n - s) + 16


def turns(eng, body, count):
    body(0)
    with eng.Fori(1, count - 1) as i:
        body(i)
    body(count - 1)


class Hidden(Units):

    def __init__(self, nc, a, table, H, dst, base, count):
        super().__init__(nc, a, 1)
        self.table, self.H, self.dst, self.base, self.count = table, H, dst, base, count
        self.bank = [a.ps(f"hp{b}", [P, 512]) for b in range(2)]
        self.act_out = [a.sb(f"hid{s}", [P, ND]) for s in range(2)]
        self.gelus = a.sem("gelus")
        self.stored = [a.sem(f"hid_stored{s}") for s in range(2)]

    def last(self, i, j):
        return isinstance(i, int) and UB * i + j >= UB * self.count

    def on_sync(self, sp, beside=lambda i, j: None):
        self.load(sp, 0, 0, self.table, self.base)
        self.load(sp, 1, 1, self.table, self.base + 1)

        def body(i):
            for j in range(UB):
                n, s = UB * i + j, j % 2
                if not self.last(i, j + 2):
                    self.load(sp, n + 2, s, self.table, n + 2 + self.base)
                beside(i, j)
                sp.wait_ge(self.gelus, n + 1)
                sp.dma_start(self.dst[bass.ds(n + self.base, 1)].rearrange("a p t -> (a p) t"),
                             self.act_out[s][:]).then_inc(self.stored[s], 16)

        turns(sp, body, self.count)
        for s in range(2):
            sp.wait_ge(self.stored[s], 16 * UB // 2 * self.count)

    def on_scalar(self, act, beside=lambda i, j: None):
        self.split_hi(act, 0, 0)

        def body(i):
            for j in range(UB):
                n, s = UB * i + j, j % 2
                if not self.last(i, j + 1):
                    self.split_hi(act, n + 1, 1 - s)
                act.wait_ge(self.done, n + 1)
                wait(act, self.stored[s], 8 * (n - s))
                self.nc.scalar.activation(self.act_out[s][:], self.bank[s][:, 0:ND], ACT.Gelu).then_inc(self.gelus, 1)
                beside(i, j)

        turns(act, body, self.count)

    def on_vector(self, vec, beside=lambda i, j: None):
        self.split_lo(vec, 0, 0)

        def body(i):
            for j in range(UB):
                if not self.last(i, j + 1):
                    self.split_lo(vec, UB * i + j + 1, (j + 1) % 2)
                beside(i, j)

        turns(vec, body, self.count)

    def on_tensor(self, pe, beside=lambda i, j: None):
        hi, lo = self.H
        mm = self.nc.tensor.matmul

        def body(i):
            for j in range(UB):
                n, s = UB * i + j, j % 2
                self.ready(pe, n)
                wait(pe, self.gelus, n - 1)
                o = self.bank[s][:, 0:ND]
                for x in range(KT):
                    mm(o, self.hi[s][:, x, :], hi[:, x, :], start=x == 0, stop=False)
                    mm(o, self.hi[s][:, x, :], lo[:, x, :], start=False, stop=False)
                    ins = mm(o, self.lo[s][:, x, :], hi[:, x, :], start=False, stop=x == KT - 1)
                ins.then_inc(self.done, 1)
                beside(i, j)

        turns(pe, body, self.count)


def route(nc, name, c, u_units, H, h_src, hidden, queries, keys, expert_ids, gates0, firsts, seconds, gates):
    HS, C2 = 2 * HEADS, TOPK * TOPK
    with ExitStack() as ctx:
        a = Alloc(nc, ctx, name)
        hid = Hidden(nc, a, u_units, H, hidden, 0, ROUTE_B)
        q = a.sb("q", [P, HS * DQ])
        ident = a.sb("ident", [P, P])
        kt = a.sb("keys", [P, HS, NKEYS])
        qT = a.sb("qT", [P, HS, P])
        s = [a.sb(f"s{n}", [P, HS, NKEYS]) for n in range(2)]
        vals = a.sb("vals", [P, HS, TOPK])
        idx = a.sb("idx", [P, HS, TOPK], U32)
        idxf = a.sb("idxf", [P, HS, TOPK])
        cand = [a.sb(f"cand{n}", [P, HEADS, C2]) for n in range(2)]
        top = a.sb("top", [P, HEADS, TOPK])
        sel = a.sb("sel", [P, HEADS, TOPK], U32)
        half = [a.sb(f"half{n}", [P, HEADS, TOPK], U32) for n in range(2)]
        halff = [a.sb(f"halff{n}", [P, HEADS, TOPK]) for n in range(2)]
        iota = a.sb("iota", [P, TOPK])
        hot = a.sb("hot", [P, HK, TOPK])
        picked = [a.sb(f"picked{n}", [P, HK]) for n in range(2)]
        gate = a.sb("gate", [P, HEADS, TOPK])
        total = a.sb("total", [P, HEADS])
        eid = a.sb("eid", [P, HK])
        tq = [a.ps(f"tq{b}", [P, 4, P]) for b in range(2)]
        sp_ = [a.ps(f"sp{b}", [P, 4, P]) for b in range(2)]
        tg = a.ps("tg", [P, 3, P])
        h_in, q_in, const_in, turned, q_copied, scored, s_copied, found, exps_in, exps = (
            a.sem(x) for x in ("h_in", "q_in", "const_in", "turned", "q_copied", "scored", "s_copied", "found", "exps_in", "exps"))
        chosen, back, kept, dstep, carried = (a.sem(x) for x in ("chosen", "back", "kept", "dstep", "carried"))
        block = ctx.enter_context(nc.Block())

        @block.sync
        def _(sp):
            sp.dma_start(ident[:], c["ident"]).then_inc(const_in, 16)
            sp.dma_start(kt[:], keys).then_inc(const_in, 16)
            sp.dma_start(iota[:], c["iota"][:, 0:TOPK]).then_inc(const_in, 16)

            def load_q(t):
                wait(sp, turned, 4 * t)
                sp.dma_start(q[:], queries[bass.ds(t * P, P), :]).then_inc(q_in, 16)

            load_q(0)
            for part, src in zip(H, h_src):
                sp.dma_start(part[:].bitcast(F32), src).then_inc(h_in, 16)

            def beside(t, j):
                if j == 0 and not hid.last(t, UB):
                    load_q(t + 1)

            hid.on_sync(sp, beside)

        @block.tensor
        def _(pe):
            pe.wait_ge(const_in, 48)

            def turn(t, b):
                if b == 0:
                    pe.wait_ge(q_in, 16 * (t + 1))
                wait(pe, q_copied, 4 * t + b - 1)
                for n in range(4):
                    ins = nc.tensor.transpose(tq[b % 2][:, n, :], q[:, (4 * b + n) * DQ:(4 * b + n + 1) * DQ], ident[:])
                ins.then_inc(turned, 1)

            def score(t, b):
                pe.wait_ge(q_copied, 4 * t + b + 1)
                wait(pe, s_copied, 4 * t + b - 1)
                for n in range(4):
                    ins = nc.tensor.matmul(sp_[b % 2][:, n, :], qT[:, 4 * b + n, :], kt[:, 4 * b + n, :], start=True,
                                           stop=True)
                ins.then_inc(scored, 1)

            def turn_back(t):
                pe.wait_ge(chosen, t + 1)
                wait(pe, kept, 3 * t)
                for n, x in enumerate((picked[0][:], picked[1][:], gate[:].rearrange("p h k -> p (h k)"))):
                    ins = nc.tensor.transpose(tg[:, n, :], x, ident[:])
                ins.then_inc(back, 1)

            for b in range(4):
                turn(0, b)
            for b in range(4):
                score(0, b)
            pe.wait_ge(h_in, 32)

            def beside(t, j):
                if not hid.last(t, UB):
                    (turn if j < 4 else score)(t + 1, j % 4)
                if j == 2 and not (isinstance(t, int) and t == 0):
                    turn_back(t - 1)

            hid.on_tensor(pe, beside)
            turn_back(TILES - 1)

        @block.scalar
        def _(act):
            def copy_q(t, b):
                act.wait_ge(turned, 4 * t + b + 1)
                wait(act, scored, 4 * t)
                nc.scalar.copy(qT[:, 4 * b:4 * b + 4, :], tq[b % 2][:]).then_inc(q_copied, 1)

            def copy_s(t, b):
                act.wait_ge(scored, 4 * t + b + 1)
                wait(act, found, t)
                nc.scalar.copy(s[0][:, 4 * b:4 * b + 4, :], sp_[b % 2][:]).then_inc(s_copied, 1)

            def keep(t):
                act.wait_ge(back, t + 1)
                for n, x in enumerate((firsts, seconds, gates)):
                    nc.scalar.copy(x[:, bass.ds(t * P, P)], tg[:, n, :]).then_inc(kept, 1)

            for b in range(4):
                copy_q(0, b)
            for b in range(4):
                copy_s(0, b)

            def beside(t, j):
                if not hid.last(t, UB):
                    (copy_q if j < 4 else copy_s)(t + 1, j % 4)
                if j == 2 and not (isinstance(t, int) and t == 0):
                    keep(t - 1)
                if j == UB - 1:
                    act.wait_ge(exps_in, t + 1)
                    nc.scalar.activation(gate[:], gate[:], ACT.Exp).then_inc(exps, 1)

            hid.on_scalar(act, beside)
            keep(TILES - 1)

        @block.vector
        def _(vec):
            d = Steps(vec, dstep)
            v, mult = nc.vector, ALU.mult
            vec.wait_ge(const_in, 48)
            pair = vals[:].rearrange("p (h s) k -> p h s k", s=2)
            ids = idxf[:].rearrange("p (h s) k -> p h s k", s=2)
            per_tile = [0]

            def ready():
                vec.sem_inc(carried, 1)

            def top16(rows, vals_of, idx_of, work, spare):
                for n in rows:
                    d(v.max(vals_of(n)[:, 0:8], work(n)))
                d.wait()
                ready()
                for n in rows:
                    d(v.max_index(idx_of(n)[:, 0:8], vals_of(n)[:, 0:8], work(n)))
                    d(v.match_replace(spare(n), vals_of(n)[:, 0:8], work(n), -3.0e38))
                d.wait()
                ready()
                for n in rows:
                    d(v.max(vals_of(n)[:, 8:16], spare(n)))
                d.wait()
                ready()
                for n in rows:
                    d(v.max_index(idx_of(n)[:, 8:16], vals_of(n)[:, 8:16], spare(n)))

            def best_keys(t, rows):
                vec.wait_ge(s_copied, 4 * t + 4)
                ready()
                top16(rows, lambda n: vals[:, n, :], lambda n: idx[:, n, :], lambda n: s[0][:, n, :], lambda n: s[1][:, n, :])
                d.wait()

            def candidates(t):
                v.tensor_scalar(idxf[:], idx[:], 1.0, None, mult).then_inc(found, 1)
                vec.wait_ge(found, t + 1)
                for h in range(HEADS):
                    d(v.tensor_tensor(cand[0][:, h, :].rearrange("p (a b) -> p a b", b=TOPK), bcast(pair[:, h, 0, :], 2, TOPK),
                                      bcast(pair[:, h, 1, :], 1, TOPK), ALU.add))
                d.wait()

            def best_pairs(rows):
                ready()
                top16(rows, lambda n: top[:, n, :], lambda n: sel[:, n, :], lambda n: cand[0][:, n, :],
                      lambda n: cand[1][:, n, :])
                d.wait()

            def pick(n):
                d(v.tensor_tensor(hot[:], bcast(halff[n][:].rearrange("p h k -> p (h k)"), 2, TOPK), bcast(iota[:], 1, HK),
                                  ALU.is_equal))
                d.wait()
                hn = hot[:].rearrange("p (h k) j -> p h k j", h=HEADS)
                d(v.tensor_tensor(hn, hn, bcast(ids[:, :, n, :], 2, TOPK), mult))
                d.wait()
                d(v.tensor_reduce(picked[n][:], hot[:], AX.X, ALU.add))
                d.wait()

            def first_keys(t):
                wait(vec, back, t)
                v.tensor_tensor(gate[:], top[:], bcast(top[:, :, 0], 2, TOPK), ALU.subtract).then_inc(exps_in, 1)
                d(v.tensor_scalar(half[0][:], sel[:], 4, None, ALU.logical_shift_right))
                d(v.tensor_scalar(half[1][:], sel[:], TOPK - 1, None, ALU.bitwise_and))
                d.wait()
                for n in range(2):
                    d(v.tensor_scalar(halff[n][:], half[n][:], 1.0, None, mult))
                d.wait()
                pick(0)

            def softmax(t):
                vec.wait_ge(exps, t + 1)
                d(v.tensor_reduce(total[:], gate[:], AX.X, ALU.add))
                d.wait()
                d(v.reciprocal(total[:], total[:]))
                d.wait()
                v.tensor_tensor(gate[:], gate[:], bcast(total[:], 2, TOPK), mult).then_inc(chosen, 1)

            def beside(t, j):
                if j == 0:
                    d.at(per_tile[0] * t)
                if j < 3:
                    best_keys(t, range(5 * j, 5 * j + 5 if j < 2 else HS))
                elif j == 3:
                    candidates(t)
                elif j < 6:
                    best_pairs(range(4 * (j - 4), 4 * (j - 3)))
                elif j == 6:
                    first_keys(t)
                else:
                    pick(1)
                if j == UB - 1 and isinstance(t, int):
                    per_tile[0] = d.n + SOFTMAX_STEPS
                if j == UB - 1:
                    softmax(t)
                    if isinstance(t, int) and t == 0:
                        vec.wait_ge(chosen, 1)
                        d(v.scalar_tensor_tensor(eid[:], picked[0][:], float(NKEYS), picked[1][:], mult, ALU.add))
                        d.wait()
                        d(v.tensor_scalar(expert_ids[:], eid[:], 1.0, None, mult))
                        d(v.tensor_scalar(gates0[:], gate[:].rearrange("p h k -> p (h k)"), 1.0, None, mult))
                        d.wait()
                        d.offset = d.n - per_tile[0]

            SOFTMAX_STEPS = 2
            hid.on_vector(vec, beside)


class Gathers:

    def __init__(self, nc, a, table, expert_ids, first, per):
        self.nc, self.table, self.ids, self.first, self.per = nc, table, expert_ids, first, per
        self.row = [a.sb(f"row{s}", [P, D]) for s in range(2)]
        self.id = [a.sb(f"id{j}", [P, 1], U32) for j in range(per)]
        self.row_in = [a.gpsimd_dma_sem(f"row_in{s}") for s in range(2)]
        self.ids_set, self.row_used, self.carried = a.sem("ids_set"), a.sem("row_used"), a.sem("gather_carried")

    def set_ids(self, pool, i):
        if not (isinstance(i, int) and i == 0):
            for s in range(2):
                pool.wait_ge(self.row_in[s], 8 * self.per * i)
        for j in range(self.per):
            self.nc.gpsimd.tensor_copy(self.id[j][:], self.ids[:, bass.ds(self.per * i + j + self.first, 1)]).then_inc(
                self.ids_set, 1)
        pool.wait_ge(self.ids_set, self.per * (i + 1))

    def gather(self, pool, i, j):
        wait(pool, self.row_used, self.per * i + j - 1)
        pool.sem_inc(self.carried, 1)
        pool.indirect_dma_start(self.row[j % 2][:], None, self.table,
                                bass.IndirectOffsetOnAxis(self.id[j][:], 0)).then_inc(self.row_in[j % 2], 16)

    def wait_row(self, vec, i, j):
        vec.wait_ge(self.row_in[j % 2], 8 * self.per * i + 16 * (j // 2 + 1))
        return self.row[j % 2]

    def dot(self, vec, i, j, rows, out):
        r = self.wait_row(vec, i, j)
        self.nc.vector.tensor_tensor_reduce(r[:], r[:], rows[:], 1.0, 0.0, ALU.mult, ALU.add, out).then_inc(self.row_used, 1)


def keep_dots(nc, vec, g, i, dot, dots, kept):
    vec.wait_ge(g.row_used, g.per * (i + 1))
    nc.vector.tensor_scalar(dots[:, bass.ds(g.per * i + g.first, g.per)], dot[:], 1.0, None, ALU.mult).then_inc(kept, 1)
    vec.wait_ge(kept, i + 1)


def gate_matrix(nc, name, c, u_units, H, hidden, u_rows, h_rows, h_rows_src, expert_ids, dots, firsts, seconds, gates, G):
    B = 4
    per_slot = 2 * GT // UB
    with ExitStack() as ctx:
        a = Alloc(nc, ctx, name)
        hid = Hidden(nc, a, u_units, H, hidden, UB * ROUTE_B, GATE_B)
        gat = Gathers(nc, a, u_rows, expert_ids, 0, UB)
        iota = a.sb("iota", [P, P])
        fcol, gcol, scol = (a.sb(n, [P, 2 * GT]) for n in ("fcol", "gcol", "scol"))
        hot1 = [a.sb(f"hot1_{n}", [P, P]) for n in range(per_slot)]
        hot2 = [a.sb(f"hot2_{n}", [P, P]) for n in range(per_slot)]
        stage = [a.sb(f"stage{n}", [P, NKEYS, GT]) for n in range(2)]
        dot = a.sb("dot", [P, UB])
        acc = [a.ps(f"acc{n}", [P, B, P]) for n in range(per_slot // B)]
        const_in, cols, seconds_col, seconds_hot, firsts_hot, made, staged, kept, carried = (
            a.sem(x) for x in ("const_in", "cols", "seconds_col", "seconds_hot", "firsts_hot", "made", "staged", "kept",
                               "carried"))
        stored = [a.sem(f"stored{n}") for n in range(2)]
        block = ctx.enter_context(nc.Block())

        @block.sync
        def _(sp):
            sp.dma_start(iota[:], c["iota"]).then_inc(const_in, 16)
            sp.dma_start(h_rows[:], h_rows_src).then_inc(const_in, 16)

            def store_group(i, x):
                sp.wait_ge(staged, 2 * UB * i + UB * (x + 1))
                sp.dma_start(G[bass.ds(2 * i + x, 1)].rearrange("g p a t -> (g p) (a t)"),
                             stage[x][:].rearrange("p a t -> p (a t)")).then_inc(stored[x], 16)

            def beside(i, j):
                if j == UB // 2 + 1:
                    store_group(i, 0)
                if j == 1 and not (isinstance(i, int) and i == 0):
                    store_group(i - 1, 1)

            hid.on_sync(sp, beside)
            store_group(GATE_B - 1, 1)
            for x in range(2):
                sp.wait_ge(stored[x], 16 * GATE_B)

        @block.gpsimd
        def _(pool):
            pool.wait_ge(const_in, 32)

            def body(i):
                gat.set_ids(pool, i)
                nc.gpsimd.tensor_copy(scol[:], seconds[:, bass.ds(2 * GT * i + DENSE0, 2 * GT)]).then_inc(seconds_col, 1)
                pool.wait_ge(seconds_col, i + 1)
                for j in range(UB):
                    gat.gather(pool, i, j)
                    wait(pool, made, 2 * (UB * i + j))
                    pool.sem_inc(carried, 1)
                    for x in range(per_slot):
                        k = per_slot * j + x
                        nc.gpsimd.tensor_scalar(hot2[x][:], iota[:], scol[:, k:k + 1], None,
                                                ALU.is_equal).then_inc(seconds_hot, 1)
                pool.wait_ge(seconds_hot, 2 * GT * (i + 1))

            turns(pool, body, GATE_B)

        @block.vector
        def _(vec):
            vec.wait_ge(const_in, 32)

            def beside(i, j):
                if j == 0:
                    wait(vec, firsts_hot, 2 * GT * i)
                    at = bass.ds(2 * GT * i + DENSE0, 2 * GT)
                    for dst, src in ((fcol, firsts), (gcol, gates)):
                        nc.vector.tensor_scalar(dst[:], src[:, at], 1.0, None, ALU.mult).then_inc(cols, 1)
                    vec.wait_ge(cols, 2 * (i + 1))
                wait(vec, made, 2 * (UB * i + j))
                for x in range(per_slot):
                    k = per_slot * j + x
                    nc.vector.tensor_scalar(hot1[x][:], iota[:], fcol[:, k:k + 1], gcol[:, k:k + 1], ALU.is_equal,
                                            ALU.mult).then_inc(firsts_hot, 1)
                gat.dot(vec, i, j, h_rows, dot[:, j:j + 1])
                if j == UB - 1:
                    keep_dots(nc, vec, gat, i, dot, dots, kept)

            hid.on_vector(vec, beside)

        @block.tensor
        def _(pe):
            def beside(i, j):
                m = UB * i + j
                for y in range(per_slot // B):
                    wait(pe, staged, 2 * (m - 1) + y + 1)
                    pe.wait_ge(seconds_hot, per_slot * m + B * (y + 1))
                    pe.wait_ge(firsts_hot, per_slot * m + B * (y + 1))
                    for x in range(B):
                        ins = nc.tensor.matmul(acc[y][:, x, :], hot2[B * y + x][:], hot1[B * y + x][:], start=True, stop=True)
                    ins.then_inc(made, 1)

            hid.on_tensor(pe, beside)

        @block.scalar
        def _(act):
            def beside(i, j):
                m, x = UB * i + j, 2 * j // UB
                if j % (UB // 2) == 0:
                    wait(act, stored[x], 16 * i)
                for y in range(per_slot // B):
                    act.wait_ge(made, 2 * m + y + 1)
                    t = per_slot * (j % (UB // 2)) + B * y
                    nc.scalar.copy(stage[x][:, :, t:t + B].rearrange("p a t -> p t a"), acc[y][:]).then_inc(staged, 1)

            hid.on_scalar(act, beside)


def gather_hidden(nc, name, u_units, H, hidden, u_rows, h_rows, expert_ids, dots, gates0):
    done = UB * GATE_B
    per = (HK - done) // GATHER_B
    assert per * GATHER_B == HK - done and per % 2 == 0
    with ExitStack() as ctx:
        a = Alloc(nc, ctx, name)
        hid = Hidden(nc, a, u_units, H, hidden, UB * (ROUTE_B + GATE_B), GATHER_B)
        gat = Gathers(nc, a, u_rows, expert_ids, done, per)
        dot = a.sb("dot", [P, per])
        kept, gelu, weighted = a.sem("kept"), a.sem("gelu"), a.sem("weighted")
        block = ctx.enter_context(nc.Block())

        @block.sync
        def _(sp):
            hid.on_sync(sp)

        @block.gpsimd
        def _(pool):
            def body(i):
                gat.set_ids(pool, i)
                for j in range(per):
                    gat.gather(pool, i, j)

            turns(pool, body, GATHER_B)

        @block.scalar
        def _(act):
            hid.on_scalar(act)
            act.wait_ge(kept, GATHER_B)
            nc.scalar.activation(dots[:], dots[:], ACT.Gelu).then_inc(gelu, 1)

        @block.vector
        def _(vec):
            def beside(i, j):
                for k in range(per * j // UB, per * (j + 1) // UB):
                    gat.dot(vec, i, k, h_rows, dot[:, k:k + 1])
                if j == UB - 1:
                    keep_dots(nc, vec, gat, i, dot, dots, kept)

            hid.on_vector(vec, beside)
            vec.wait_ge(gelu, 1)
            nc.vector.tensor_tensor(dots[:], dots[:], gates0[:], ALU.mult).then_inc(weighted, 1)
            vec.wait_ge(weighted, 1)

        @block.tensor
        def _(pe):
            hid.on_tensor(pe)


def outputs(nc, name, v_units, hidden, G, v_rows, expert_ids, dots, acc, accg):
    mult = ALU.mult
    with ExitStack() as ctx:
        a = Alloc(nc, ctx, name)
        un = Units(nc, a, 4)
        gat = Gathers(nc, a, v_rows, expert_ids, 0, 2 * DS)
        W = [a.sb(f"w{s}", [P, CH, ND]) for s in range(2)]
        Gc = [a.sb(f"g{s}", [P, NG, CH, GT]) for s in range(2)]
        W_hi = [a.sb(f"w_hi{s}", [P, CH, ND], F32R) for s in range(2)]
        W_lo = [a.sb(f"w_lo{s}", [P, CH, ND], F32R) for s in range(2)]
        w8 = a.sb("w8", [P, gat.per])
        vp = [[a.ps(f"vp{s}_{b}", [P, 512]) for b in range(4)] for s in range(2)]
        weighed = a.sem("weighed")
        added, gated, w_hi_done, w_lo_done, w_set, cleared = (
            a.sem(x) for x in ("added", "gated", "w_hi_done", "w_lo_done", "w_set", "cleared"))
        w_in = [a.sem(f"w_in{s}") for s in range(2)]
        block = ctx.enter_context(nc.Block())

        T = NCH // 2

        def unit(i, s, j):
            return DS * (2 * i + s) + j

        def is_last(i, s):
            return isinstance(i, int) and 2 * i + s == NCH - 1

        @block.sync
        def _(sp):
            def load_w(i, s):
                wait(sp, w_lo_done, 2 * (i - 1) + s + 1)
                at = bass.ds(CH * (2 * i + s), CH)
                sp.dma_start(W[s][:], hidden[at].rearrange("a p t -> p a t")).then_inc(w_in[s], 16)
                sp.dma_start(Gc[s][:].rearrange("p g a t -> p g (a t)"),
                             G[:, :, at, :].rearrange("g p a t -> p g (a t)")).then_inc(w_in[s], 16)

            def body(i):
                for s in range(2):
                    for j in range(DS):
                        n = unit(i, s, j)
                        if not (is_last(i, s) and j >= DS - 2):
                            un.load(sp, n + 2, j % 2, v_units, n + 2)
                        if j == 0 and not (isinstance(i, int) and i == T - 1):
                            load_w(i + 1, s)

            load_w(0, 0)
            for n in range(2):
                un.load(sp, n, n, v_units, n)
            load_w(0, 1)
            turns(sp, body, T)

        @block.gpsimd
        def _(pool):
            def body(i):
                gat.set_ids(pool, i)
                for j in range(gat.per):
                    gat.gather(pool, i, j)

            turns(pool, body, T)

        @block.scalar
        def _(act):
            def weights_hi(i, s):
                act.wait_ge(gated, 2 * i + s + 1)
                wait(act, un.done, 4 * DS * (2 * i + s - 1))
                nc.scalar.copy(W_hi[s][:], W[s][:]).then_inc(w_hi_done, 1)

            def body(i):
                for s in range(2):
                    for j in range(DS):
                        if not (is_last(i, s) and j == DS - 1):
                            un.split_hi(act, unit(i, s, j) + 1, (j + 1) % 2)
                        if j == 1 and not is_last(i, s):
                            weights_hi(*((i, 1) if s == 0 else (i + 1, 0)))

            un.split_hi(act, 0, 0)
            weights_hi(0, 0)
            turns(act, body, T)

        @block.vector
        def _(vec):
            v = nc.vector

            def weigh(i, s):
                vec.wait_ge(w_in[s], 32 * (i + 1))
                w = W[s][:].rearrange("p a (g t) -> p a g t", t=GT)
                for e in range(CH):
                    ins = v.tensor_tensor(w[:, e], w[:, e], Gc[s][:, :, e, :], mult)
                    if e < CH - 1:
                        ins.then_inc(weighed, 1)
                ins.then_inc(gated, 1)

            def weights_lo(i, s):
                vec.wait_ge(w_hi_done, 2 * i + s + 1)
                v.tensor_tensor(W_lo[s][:], W[s][:], W_hi[s][:].bitcast(F32), ALU.subtract).then_inc(w_lo_done, 1)

            def add(i, s, j, b):
                k = 4 * unit(i, s, j) + b
                vec.wait_ge(un.done, k + 1)
                wait(vec, added, k + 1 - 4 * DS)
                o = acc[:, 4 * j + b, :]
                v.tensor_tensor(o, o, vp[j % 2][b][:, 0:ND], ALU.add).then_inc(added, 1)

            def gathered(i, j):
                r = gat.wait_row(vec, i, j)
                wait(vec, gat.row_used, gat.per * i + j)
                v.scalar_tensor_tensor(accg[:], r[:], w8[:, j:j + 1], accg[:], mult, ALU.add).then_inc(gat.row_used, 1)

            def body(i):
                wait(vec, gat.row_used, gat.per * i)
                v.tensor_scalar(w8[:], dots[:, bass.ds(gat.per * i, gat.per)], 1.0, None, mult).then_inc(w_set, 1)
                vec.wait_ge(w_set, i + 1)
                for s in range(2):
                    for j in range(DS):
                        if not (is_last(i, s) and j == DS - 1):
                            un.split_lo(vec, unit(i, s, j) + 1, (j + 1) % 2)
                        nxt = (i, 1) if s == 0 else (i + 1, 0)
                        if j == 0 and not is_last(i, s):
                            weigh(*nxt)
                        if j == 2 and not is_last(i, s):
                            weights_lo(*nxt)
                        add(i, s, j, 0)
                        add(i, s, j, 1)
                        gathered(i, DS * s + j)
                        add(i, s, j, 2)
                        add(i, s, j, 3)

            v.memset(acc[:], 0.0).then_inc(cleared, 1)
            v.memset(accg[:], 0.0).then_inc(cleared, 1)
            un.split_lo(vec, 0, 0)
            weigh(0, 0)
            weights_lo(0, 0)
            vec.wait_ge(cleared, 2)
            turns(vec, body, T)

        @block.tensor
        def _(pe):
            mm = nc.tensor.matmul

            def body(i):
                for s in range(2):
                    for j in range(DS):
                        n = unit(i, s, j)
                        un.ready(pe, n)
                        if j == 0:
                            pe.wait_ge(w_lo_done, 2 * i + s + 1)
                        x = j % 2
                        for b in range(4):
                            wait(pe, added, 4 * (n - 2) + b + 1)
                            o = vp[x][b][:, 0:ND]
                            for e in range(CH):
                                hi, lo = un.hi[x][:, 4 * e + b, :], un.lo[x][:, 4 * e + b, :]
                                mm(o, hi, W_hi[s][:, e, :], start=e == 0, stop=False)
                                mm(o, hi, W_lo[s][:, e, :], start=False, stop=False)
                                ins = mm(o, lo, W_hi[s][:, e, :], start=False, stop=e == CH - 1)
                            ins.then_inc(un.done, 1)

            turns(pe, body, T)


def finish(nc, name, c, sums, w_row, acc, accg, y):
    with ExitStack() as ctx:
        a = Alloc(nc, ctx, name)
        X = [a.sb(f"x{t}", [P, D]) for t in range(TILES)]
        W = a.sb("w", [P, D])
        junk = a.sb("junk", [P, D])
        ident = a.sb("ident", [P, P])
        mean, root, rstd, tmp, ss = (a.sb(n, [P, TILES]) for n in ("mean", "root", "rstd", "tmp", "ss"))
        bank = [a.ps(f"t{b}", [P, 4, P]) for b in range(4)]
        loaded = [a.sem(f"loaded{t}") for t in range(TILES)]
        const_in, turned, summed, squared, meaned, rooted, scaled, done, stored, dstep, half_added = (
            a.sem(s) for s in ("const_in", "turned", "summed", "squared", "meaned", "rooted", "scaled", "done", "stored",
                               "dstep", "half_added"))
        block = ctx.enter_context(nc.Block())

        def rows(t):
            return P if t < PTILES else NSMP

        @block.sync
        def _(sp):
            sp.dma_start(ident[:], c["ident"]).then_inc(const_in, 16)
            sp.dma_start(W[:], w_row.partition_broadcast(P)).then_inc(const_in, 16)
            for t in range(TILES):
                sp.dma_start(X[t][:], sums[t * P:(t + 1) * P, :]).then_inc(loaded[t], 16)
            for t in range(TILES):
                sp.wait_ge(done, t + 1)
                sp.dma_start(y[t * P:t * P + rows(t), :], X[t][0:rows(t), :]).then_inc(stored, 16)
            sp.wait_ge(stored, 16 * TILES)

        @block.tensor
        def _(pe):
            pe.wait_ge(const_in, 32)
            for t in range(1, TILES):
                R = rows(t)
                for b in range(4):
                    wait(pe, half_added, 4 * (t - 2) + b + 1)
                    for k in range(4):
                        ins = nc.tensor.transpose(bank[b][0:R, k, :], acc[:, 4 * b + k, (t - 1) * P:(t - 1) * P + R], ident[:])
                    ins.then_inc(turned, 1)

        @block.scalar
        def _(act):
            for t in range(TILES):
                R = rows(t)
                if t == 0:
                    act.wait_ge(summed, 1)
                else:
                    act.wait_ge(half_added, 4 * t)
                wait(act, squared, t)
                nc.scalar.activation(junk[0:R, :], X[t][0:R, :], ACT.Square, accum_out=ss[0:R, t:t + 1]).then_inc(squared, 1)
                act.wait_ge(meaned, t + 1)
                nc.scalar.activation(root[0:R, t:t + 1], mean[0:R, t:t + 1], ACT.Sqrt).then_inc(rooted, 1)

        @block.vector
        def _(vec):
            v, d = nc.vector, Steps(vec, dstep)
            vec.wait_ge(const_in, 32)

            def add(t):
                R = rows(t)
                vec.wait_ge(loaded[t], 16)
                if t == 0:
                    v.tensor_tensor(X[0][:], X[0][:], accg[:], ALU.add).then_inc(summed, 1)
                    return
                for b in range(4):
                    vec.wait_ge(turned, 4 * (t - 1) + b + 1)
                    x = X[t][0:R, 512 * b:512 * (b + 1)].rearrange("p (k f) -> p k f", k=4)
                    v.tensor_tensor(x, x, bank[b][0:R], ALU.add).then_inc(half_added, 1)

            def norm(t):
                R, at = rows(t), slice(t, t + 1)
                vec.wait_ge(squared, t + 1)
                v.tensor_scalar(mean[0:R, at], ss[0:R, at], 1.0 / D, EPS, ALU.mult, ALU.add).then_inc(meaned, 1)
                vec.wait_ge(meaned, t + 1)
                vec.wait_ge(rooted, t + 1)
                newton_rsqrt(nc, d, rstd[0:R, at], mean[0:R, at], root[0:R, at], tmp[0:R, at])
                v.scalar_tensor_tensor(X[t][0:R, :], X[t][0:R, :], rstd[0:R, at], W[0:R, :], ALU.mult,
                                       ALU.mult).then_inc(done, 1)

            add(0)
            for t in range(1, TILES):
                add(t)
                norm(t - 1)
            norm(TILES - 1)


def build(nc, x, w, consts, keys, tables, states, outs):
    def scratch(name, shape):
        return nc.dram_tensor(name, shape, F32, kind="Internal").ap()

    proj, alr = scratch("proj", (TP, PROJ)), scratch("alr", (RANK, TP))
    mix, sums = scratch("mix", (TP, D)), scratch("sums", (TP, D))
    queries, h_rows = scratch("queries", (TP, D)), scratch("h_rows", (P, D))
    h_hi, h_lo = scratch("h_hi", (P, KT, TP)), scratch("h_lo", (P, KT, TP))
    hidden, G = scratch("hidden", (NKEYS, P, ND)), scratch("gate_mat", (NG, P, NKEYS, GT))
    ident = consts["ident"]

    def parts(ctx, n):
        return [ctx.enter_context(nc.sbuf_tensor(f"rows{n}_{p}", [P, KT, TP], F32R)) for p in ("hi", "lo")]

    with ExitStack() as ctx:
        hi, lo = parts(ctx, 1)
        weights = Weights(nc, ctx, "w_in", w["in"], small=w["alr"])
        norm_transpose(nc, "norm1", hi, lo, ident, x, weights, norm=w["norm_mix"])
        stream_matmul(nc, "in_proj", hi, lo, weights, proj, small=alr)
    mixer(nc, "mixer", consts, proj, alr, w["a2"], w["gn"], states, outs["states"], mix)
    with ExitStack() as ctx:
        hi, lo = parts(ctx, 2)
        weights = Weights(nc, ctx, "w_out", w["out"])
        norm_transpose(nc, "turn_mix", hi, lo, ident, mix, weights)
        stream_matmul(nc, "out_proj", hi, lo, weights, sums, residual=x)
    with ExitStack() as ctx:
        hi, lo = parts(ctx, 3)
        weights = Weights(nc, ctx, "w_pq", w["pq"])
        norm_transpose(nc, "norm2", hi, lo, ident, sums, weights, norm=w["norm_ffn"], row=h_rows)
        stream_matmul(nc, "queries", hi, lo, weights, queries, spill=(h_hi, h_lo))
    with ExitStack() as ctx:
        def sb(name, shape, dt=F32, on=ctx):
            return on.enter_context(nc.sbuf_tensor(name, shape, dt))

        expert_ids, gates0, dots = sb("expert_ids", [P, HK], U32), sb("gates0", [P, HK]), sb("dots", [P, HK])
        with ExitStack() as inner:
            H = [sb(f"dense_{p}", [P, KT, ND], F32R, inner) for p in ("hi", "lo")]
            choices = [sb(n, [P, TP], on=inner) for n in ("firsts", "seconds", "gates")]
            dense = slice(DENSE0, DENSE0 + ND)
            route(nc, "route", consts, tables["u_units"], H, (h_hi[:, :, dense], h_lo[:, :, dense]), hidden, queries, keys,
                  expert_ids, gates0, *choices)
            rows0 = sb("rows0", [P, D], on=inner)
            gate_matrix(nc, "gate_matrix", consts, tables["u_units"], H, hidden, tables["u_rows"], rows0, h_rows,
                        expert_ids, dots, *choices, G)
            gather_hidden(nc, "gather_hidden", tables["u_units"], H, hidden, tables["u_rows"], rows0, expert_ids, dots, gates0)
        acc, accg = sb("acc", [P, KT, ND]), sb("accg", [P, D])
        outputs(nc, "outputs", tables["v_units"], hidden, G, tables["v_rows"], expert_ids, dots, acc, accg)
        finish(nc, "finish", consts, sums, w["norm_final"], acc, accg, outs["y"])


def kernel(**inputs):
    import concourse.bacc as bacc
    from concourse.bass_utils import run_bass_kernel_spmd

    nc = bacc.Bacc("TRN2", target_bir_lowering=False, num_devices=1)
    g = {k: np.asarray(v) for k, v in inputs.items()}
    arrays = {}

    def put(name, array):
        arrays[name] = np.ascontiguousarray(array)
        return nc.dram_tensor(name, arrays[name].shape, mybir.dt.from_np(arrays[name].dtype), kind="ExternalInput").ap()

    def out(name, shape):
        return nc.dram_tensor(name, shape, F32, kind="ExternalOutput").ap()

    def blocks(m):
        return m.reshape(KQ, KT // KQ, P, -1, NB).transpose(3, 0, 2, 1, 4)

    x = np.zeros((TP, D), np.float32)
    x[:SEQ] = g["x_prompt"][0]
    x[SEQ:SEQ + NSMP] = g["x_sample"].reshape(NSMP, D)
    alr = np.zeros((D, P), np.float32)
    alr[:, :RANK] = g["w_in"][0][:, PROJ:]
    w = {
        "norm_mix": put("norm_mix", g["w_norm_mix"][0]),
        "norm_ffn": put("norm_ffn", g["w_norm_ffn"][0]),
        "norm_final": put("norm_final", g["w_norm_final"]),
        "in": put("w_in", blocks(g["w_in"][0][:, :PROJ])),
        "alr": put("w_alr", alr.reshape(KT, P, P).transpose(1, 0, 2)),
        "out": put("w_out", blocks(g["w_out"][0])),
        "pq": put("w_pq", blocks(g["w_pq"][0])),
        "a2": put("w_a2", np.concatenate([g["w_gla_a2"][0], g["b_gla_a"][0][None]], 0)),
        "gn": put("gn", np.stack([g["gn_ret_w"][0].ravel(), g["gn_ret_b"][0].ravel(), g["gn_gla_w"][0].ravel()])),
    }
    keys = np.stack([g["sub_keys1"][0], g["sub_keys2"][0]], 1)
    keys = put("keys", keys.reshape(2 * HEADS, NKEYS, DQ).transpose(2, 0, 1))
    u, v = g["u_tab"][0], g["v_tab"][0]
    tables = {
        "u_rows": put("u_rows", u),
        "v_rows": put("v_rows", v),
        "u_units": put("u_units", u.reshape(NKEYS, NKEYS, KT, P).transpose(0, 3, 2, 1).reshape(NKEYS, P, D)),
        "v_units": put("v_units", v.reshape(NCH, CH, NKEYS, DS, 512).transpose(0, 3, 2, 1, 4).reshape(NCH * DS, P, D)),
    }
    consts = {k: put(f"const_{k}", a) for k, a in constants().items()}
    states = (put("state_ret", g["state_ret"][0]), put("state_gla", g["state_gla"][0]))
    outs = {
        "y": out("y", (SEQ + NSMP, D)),
        "states": [[out("ret_p", (H, DK, DV)), out("gla_p", (H, DK, DV))],
                   [out("ret_s", (NSEQ, H, DK, DV)), out("gla_s", (NSEQ, H, DK, DV))]],
    }
    build(nc, put("x", x), w, consts, keys, tables, states, outs)
    r = run_bass_kernel_spmd(nc, [arrays], core_ids=[0]).results[0]
    y = r["y"]
    return (y[:SEQ].reshape(1, SEQ, D), y[SEQ:].reshape(NSEQ, LSEQ, D), r["ret_p"].reshape(1, 1, H, DK, DV),
            r["gla_p"].reshape(1, 1, H, DK, DV), r["ret_s"].reshape(1, NSEQ, H, DK, DV),
            r["gla_s"].reshape(1, NSEQ, H, DK, DV))
```
